# Optimizing a Trainium2 kernel written in Bass

```python
import math, functools
import jax, jax.numpy as jnp
from jax import lax
import numpy as np

D_MODEL = 1024
BATCH = 1
SEQ = 512
DEPTH = 2
DEC_BATCH = 8
DEC_SEQ = 8
PAST_LEN = 512
PAGE_SIZE = 128

N_A_LAYERS = DEPTH // 2
N_B_LAYERS = DEPTH - N_A_LAYERS
HGRN_EXPAND = 128
HGRN_HEADS = D_MODEL // HGRN_EXPAND
HGRN_DK = HGRN_EXPAND
HGRN_DV = D_MODEL // HGRN_HEADS
HGRN_FD = HGRN_HEADS * HGRN_DK
HGRN_CHUNK = 64
FOX_HEAD_DIM = 64
FOX_HEADS = D_MODEL // FOX_HEAD_DIM
FOX_SCALE = FOX_HEAD_DIM ** -0.5
Q_BLOCK = 128
D_FF = ((8 * D_MODEL // 3 + 127) // 128) * 128
CONV_W = 3
EPS = 1e-6

kernel_name = "yoco_hgrn2_fox_convffn_step"

def rmsnorm(x, g):
    xf = x.astype(jnp.float32)
    r = lax.rsqrt(jnp.mean(xf * xf, axis=-1, keepdims=True) + EPS)
    return (xf * r).astype(x.dtype) * g

def hgrn2_recurrence(q, k, logf, v, s0):
    B, T, H, DK = q.shape
    C = math.gcd(T, HGRN_CHUNK)
    n = T // C
    f32 = jnp.float32

    def to_chunks(a):
        return a.astype(f32).reshape(B, n, C, H, a.shape[-1]).transpose(1, 0, 3, 2, 4)

    tri = jnp.tril(jnp.ones((C, C), dtype=bool))[:, :, None]

    def step(S, xs):
        qc, kc, lc, vc = xs
        b = jnp.cumsum(lc, axis=2)
        diff = b[:, :, :, None, :] - b[:, :, None, :, :]
        decay = jnp.where(tri, jnp.exp(jnp.where(tri, diff, 0.0)), 0.0)
        A = jnp.einsum('bhtd,bhsd,bhtsd->bhts', qc, kc, decay)
        o = (jnp.einsum('bhts,bhsv->bhtv', A, vc)
             + jnp.einsum('bhtd,bhdv->bhtv', qc * jnp.exp(b), S))
        b_last = b[:, :, -1:, :]
        S = (jnp.exp(b_last[:, :, 0, :])[..., None] * S
             + jnp.einsum('bhsd,bhsv->bhdv', kc * jnp.exp(b_last - b), vc))
        return S, o

    S, o = lax.scan(step, s0.astype(f32), (to_chunks(q), to_chunks(k), to_chunks(logf), to_chunks(v)))
    o = o.transpose(1, 0, 3, 2, 4).reshape(B, T, H, -1)
    return o, S

def hgrn2_mixer(h, s0, w_in, lb, g_onorm, w_o, first_layer):
    B, T, _ = h.shape
    proj = h @ w_in
    q, fr, i, g = jnp.split(proj, [HGRN_FD, 2 * HGRN_FD, 2 * HGRN_FD + D_MODEL], axis=-1)
    q = jax.nn.silu(q)
    fr = fr.astype(jnp.float32)
    if first_layer:
        logf = jax.nn.log_sigmoid(fr)
        k = jax.nn.sigmoid(-fr)
    else:
        lb = lb.astype(jnp.float32)
        f = lb + (1.0 - lb) * jax.nn.sigmoid(fr)
        logf = jnp.log(f)
        k = (1.0 - lb) * jax.nn.sigmoid(-fr)
    heads = lambda a, d: a.reshape(B, T, HGRN_HEADS, d)
    o, S = hgrn2_recurrence(heads(q, HGRN_DK), heads(k, HGRN_DK), heads(logf, HGRN_DK),
                            heads(i, HGRN_DV), s0)
    o = rmsnorm(o.astype(h.dtype), g_onorm).reshape(B, T, D_MODEL) * jax.nn.silu(g)
    return o @ w_o, S

def conv_ffn(h, conv_prev, w_in, conv_w, conv_b, w_out):
    T = h.shape[1]
    u, gate = jnp.split(h @ w_in, 2, axis=-1)
    ext = jnp.concatenate([conv_prev.astype(u.dtype), u], axis=1)
    a = conv_b + sum(ext[:, j:j + T] * conv_w[j] for j in range(CONV_W))
    out = (jax.nn.silu(a) * gate) @ w_out
    return out, ext[:, -(CONV_W - 1):]

def shared_kv(h, kv_norm, w_kvf, b_f, k_norm):
    B, T, _ = h.shape
    hn = rmsnorm(h, kv_norm)
    k, v, fl = jnp.split(hn @ w_kvf, [D_MODEL, 2 * D_MODEL], axis=-1)
    k = rmsnorm(k.reshape(B, T, FOX_HEADS, FOX_HEAD_DIM), k_norm)
    v = v.reshape(B, T, FOX_HEADS, FOX_HEAD_DIM)
    logf = jax.nn.log_sigmoid((fl + b_f).astype(jnp.float32))
    return k, v, logf

def fox_block_attention(q, k, v, cum):
    B, S, H, D = q.shape
    nb = S // Q_BLOCK
    qb = q.reshape(B, nb, Q_BLOCK, H, D).transpose(1, 0, 2, 3, 4)
    cqb = cum.reshape(B, nb, Q_BLOCK, H).transpose(1, 0, 3, 2)
    qpos = jnp.arange(S).reshape(nb, Q_BLOCK)
    kpos = jnp.arange(S)
    cum_k = cum.transpose(0, 2, 1)

    def one_block(args):
        qi, cqi, pi = args
        s = jnp.einsum('bqhd,bkhd->bhqk', qi, k).astype(jnp.float32) * FOX_SCALE
        logits = s + (cqi[..., :, None] - cum_k[..., None, :])
        mask = kpos[None, :] <= pi[:, None]
        p = jax.nn.softmax(jnp.where(mask, logits, -jnp.inf), axis=-1)
        return jnp.einsum('bhqk,bkhd->bqhd', p.astype(v.dtype), v)

    out = lax.map(one_block, (qb, cqb, qpos))
    return out.transpose(1, 0, 2, 3, 4).reshape(B, S, H, D)

def fox_decode_attention(q, k_new, v_new, c_new, k_past, v_past, c_past):
    T = q.shape[1]
    P = k_past.shape[1]
    cq = c_new.transpose(0, 2, 1)
    s_past = (jnp.einsum('bqhd,bkhd->bhqk', q, k_past).astype(jnp.float32) * FOX_SCALE
              + (cq[..., :, None] - c_past.transpose(0, 2, 1)[..., None, :]))
    s_new = (jnp.einsum('bqhd,bkhd->bhqk', q, k_new).astype(jnp.float32) * FOX_SCALE
             + (cq[..., :, None] - cq[..., None, :]))
    tri = jnp.tril(jnp.ones((T, T), dtype=bool))
    s_new = jnp.where(tri, s_new, -jnp.inf)
    p = jax.nn.softmax(jnp.concatenate([s_past, s_new], axis=-1), axis=-1)
    return (jnp.einsum('bhqk,bkhd->bqhd', p[..., :P].astype(v_past.dtype), v_past)
            + jnp.einsum('bhqk,bkhd->bqhd', p[..., P:].astype(v_new.dtype), v_new))

def run_trunk(x, hgrn_s0, conv_s0, past, norm_mix, norm_ffn, hgrn_w_in, hgrn_lb_param, hgrn_onorm,
              hgrn_w_o, kv_norm, w_kvf, fox_b_f, k_norm, fox_w_qg, q_norm, fox_w_o,
              ffn_w_in, ffn_conv_w, ffn_conv_b, ffn_w_out):
    B, T, _ = x.shape
    p = jax.nn.softmax(hgrn_lb_param.astype(jnp.float32), axis=0)
    lower_bounds = jnp.cumsum(p, axis=0) - p[0]
    h = x
    new_hgrn, new_conv = [], []
    k = v = logf = c_new = c_past = k_past = v_past = None
    for layer in range(DEPTH):
        hn = rmsnorm(h, norm_mix[layer])
        if layer < N_A_LAYERS:
            mix, S = hgrn2_mixer(hn, hgrn_s0[layer], hgrn_w_in[layer], lower_bounds[layer],
                                 hgrn_onorm[layer], hgrn_w_o[layer], first_layer=(layer == 0))
            new_hgrn.append(S)
        else:
            j = layer - N_A_LAYERS
            qg = hn @ fox_w_qg[j]
            q, gate = jnp.split(qg, 2, axis=-1)
            q = rmsnorm(q.reshape(B, T, FOX_HEADS, FOX_HEAD_DIM), q_norm[j])
            if past is None:
                o = fox_block_attention(q, k, v, c_new)
            else:
                o = fox_decode_attention(q, k, v, c_new, k_past, v_past, c_past)
            mix = (o.reshape(B, T, D_MODEL) * jax.nn.sigmoid(gate)) @ fox_w_o[j]
        h = h + mix
        f, cs = conv_ffn(rmsnorm(h, norm_ffn[layer]), conv_s0[layer], ffn_w_in[layer],
                         ffn_conv_w[layer], ffn_conv_b[layer], ffn_w_out[layer])
        new_conv.append(cs)
        h = h + f
        if layer == N_A_LAYERS - 1:
            k, v, logf = shared_kv(h, kv_norm, w_kvf, fox_b_f, k_norm)
            if past is None:
                c_new = jnp.cumsum(logf, axis=1)
            else:
                k_past, v_past, logf_past = past
                P = logf_past.shape[1]
                c_all = jnp.cumsum(jnp.concatenate([logf_past.astype(jnp.float32), logf], axis=1), axis=1)
                c_past, c_new = c_all[:, :P], c_all[:, P:]
    return h, k, v, logf, jnp.stack(new_hgrn), jnp.stack(new_conv)

def setup_inputs(seed: int = 0) -> dict:
    key = jax.random.key(seed)
    ks = jax.random.split(key, 32)
    f32 = jnp.float32
    n_pages = PAST_LEN // PAGE_SIZE
    n_used = DEC_BATCH * n_pages
    n_phys = n_used + max(1, n_used // 4)

    def nrm(k, shape, s=1.0):
        return s * jax.random.normal(k, shape, f32)

    def gain(k, shape):
        return 1.0 + 0.05 * jax.random.normal(k, shape, f32)

    d_inv = D_MODEL ** -0.5
    x_prompt = nrm(ks[0], (BATCH, SEQ, D_MODEL))
    x_sample = nrm(ks[1], (DEC_BATCH, DEC_SEQ, D_MODEL))
    cache_k = nrm(ks[2], (n_phys, PAGE_SIZE, FOX_HEADS, FOX_HEAD_DIM))
    cache_v = nrm(ks[3], (n_phys, PAGE_SIZE, FOX_HEADS, FOX_HEAD_DIM))
    cache_logf = jax.nn.log_sigmoid(jax.random.uniform(ks[4], (n_phys, PAGE_SIZE, FOX_HEADS), f32, 2.0, 6.0))
    state_hgrn = nrm(ks[5], (N_A_LAYERS, DEC_BATCH, HGRN_HEADS, HGRN_DK, HGRN_DV), 0.5)
    state_conv = nrm(ks[6], (DEPTH, DEC_BATCH, CONV_W - 1, D_FF))
    page_table = jax.random.permutation(ks[7], n_phys)[:n_used].reshape(DEC_BATCH, n_pages).astype(jnp.int32)

    norm_mix = gain(ks[8], (DEPTH, D_MODEL))
    norm_ffn = gain(ks[9], (DEPTH, D_MODEL))
    hgrn_w_in = nrm(ks[10], (N_A_LAYERS, D_MODEL, 2 * HGRN_FD + 2 * D_MODEL), d_inv)
    hgrn_lb_param = nrm(ks[11], (N_A_LAYERS, HGRN_FD))
    hgrn_onorm = gain(ks[12], (N_A_LAYERS, HGRN_DV))
    hgrn_w_o = nrm(ks[13], (N_A_LAYERS, D_MODEL, D_MODEL), d_inv)
    kv_norm = gain(ks[14], (D_MODEL,))
    w_kvf = jnp.concatenate([nrm(ks[15], (D_MODEL, 2 * D_MODEL), d_inv),
                             nrm(ks[16], (D_MODEL, FOX_HEADS), 0.3 * d_inv)], axis=1)
    fox_b_f = jax.random.uniform(ks[17], (FOX_HEADS,), f32, 2.0, 6.0)
    k_norm = gain(ks[18], (FOX_HEAD_DIM,))
    fox_w_qg = nrm(ks[19], (N_B_LAYERS, D_MODEL, 2 * D_MODEL), d_inv)
    q_norm = gain(ks[20], (N_B_LAYERS, FOX_HEAD_DIM))
    fox_w_o = nrm(ks[21], (N_B_LAYERS, D_MODEL, D_MODEL), d_inv)
    ffn_w_in = nrm(ks[22], (DEPTH, D_MODEL, 2 * D_FF), d_inv)
    ffn_conv_w = nrm(ks[23], (DEPTH, CONV_W, D_FF), CONV_W ** -0.5)
    ffn_conv_b = nrm(ks[24], (DEPTH, D_FF), 0.02)
    ffn_w_out = nrm(ks[25], (DEPTH, D_FF, D_MODEL), D_FF ** -0.5)
    return {"x_prompt": x_prompt, "x_sample": x_sample, "cache_k": cache_k, "cache_v": cache_v,
            "cache_logf": cache_logf, "state_hgrn": state_hgrn, "state_conv": state_conv,
            "page_table": page_table, "norm_mix": norm_mix, "norm_ffn": norm_ffn,
            "hgrn_w_in": hgrn_w_in, "hgrn_lb_param": hgrn_lb_param, "hgrn_onorm": hgrn_onorm,
            "hgrn_w_o": hgrn_w_o, "kv_norm": kv_norm, "w_kvf": w_kvf, "fox_b_f": fox_b_f,
            "k_norm": k_norm, "fox_w_qg": fox_w_qg, "q_norm": q_norm, "fox_w_o": fox_w_o,
            "ffn_w_in": ffn_w_in, "ffn_conv_w": ffn_conv_w, "ffn_conv_b": ffn_conv_b,
            "ffn_w_out": ffn_w_out}

def reference(x_prompt, x_sample, cache_k, cache_v, cache_logf, state_hgrn, state_conv, page_table,
              norm_mix, norm_ffn, hgrn_w_in, hgrn_lb_param, hgrn_onorm, hgrn_w_o, kv_norm, w_kvf,
              fox_b_f, k_norm, fox_w_qg, q_norm, fox_w_o, ffn_w_in, ffn_conv_w, ffn_conv_b, ffn_w_out):
    trunk = functools.partial(
        run_trunk, norm_mix=norm_mix, norm_ffn=norm_ffn, hgrn_w_in=hgrn_w_in,
        hgrn_lb_param=hgrn_lb_param, hgrn_onorm=hgrn_onorm, hgrn_w_o=hgrn_w_o, kv_norm=kv_norm,
        w_kvf=w_kvf, fox_b_f=fox_b_f, k_norm=k_norm, fox_w_qg=fox_w_qg, q_norm=q_norm,
        fox_w_o=fox_w_o, ffn_w_in=ffn_w_in, ffn_conv_w=ffn_conv_w, ffn_conv_b=ffn_conv_b,
        ffn_w_out=ffn_w_out)

    B = x_prompt.shape[0]
    hgrn0 = jnp.zeros((N_A_LAYERS, B, HGRN_HEADS, HGRN_DK, HGRN_DV), jnp.float32)
    conv0 = jnp.zeros((DEPTH, B, CONV_W - 1, D_FF), x_prompt.dtype)
    y_prompt, k_prompt, v_prompt, logf_prompt, hgrn_prompt, conv_prompt = trunk(
        x_prompt, hgrn0, conv0, None)

    Bd, n_pages = page_table.shape
    page = cache_k.shape[1]
    k_past = cache_k[page_table].reshape(Bd, n_pages * page, FOX_HEADS, FOX_HEAD_DIM)
    v_past = cache_v[page_table].reshape(Bd, n_pages * page, FOX_HEADS, FOX_HEAD_DIM)
    logf_past = cache_logf[page_table].reshape(Bd, n_pages * page, FOX_HEADS)
    y_sample, k_sample, v_sample, logf_sample, hgrn_sample, conv_sample = trunk(
        x_sample, state_hgrn, state_conv, (k_past, v_past, logf_past))

    return (y_prompt, y_sample, k_prompt, v_prompt, logf_prompt, k_sample, v_sample, logf_sample,
            hgrn_prompt, hgrn_sample, conv_prompt, conv_sample)


_drawn_inputs = setup_inputs


def setup_inputs(seed=0):
    import zlib

    import numpy as np

    out = dict(_drawn_inputs(seed))
    spreads = {}
    factors = {'cache_logf': 6.733, 'q_norm': 8.0, 'ffn_conv_b': 4.376}
    for name, (base, spread) in spreads.items():
        noise = np.random.default_rng([zlib.crc32(name.encode()), seed]).standard_normal(out[name].shape)
        drawn = base * np.exp(spread * noise) if base else spread * noise
        out[name] = __import__('jax').numpy.asarray(drawn.astype(out[name].dtype))
    for name, factor in factors.items():
        out[name] = (out[name] * factor).astype(out[name].dtype)
    return out
```

```python
from contextlib import ExitStack

import concourse.bass as bass
from concourse import mybir

F32 = mybir.dt.float32
F32R = mybir.dt.float32r
BF16 = mybir.dt.bfloat16
U8 = mybir.dt.uint8
I32 = mybir.dt.int32
ALU = mybir.AluOpType
ACT = mybir.ActivationFunctionType
AX = mybir.AxisListType

P = 128
SEQ = 512
NSEQ = 8
DSEQ = 8
NS = NSEQ * DSEQ
T = SEQ + NS
HALF = T // 2
DT = 8
FT = 22
HEADS = 8
FOX = 16
CH = 128
NCH = SEQ // CH
PAGES = 4
EPS = 1e-6
LEVELS = [64, 32, 16, 8, 4, 2, 1]
SAMPLE_GRAM = {3: 0, 5: 5, 6: 6, 7: 7}
RAW = 4
SPL = 2
FO_K = [list(range(0, 8)), list(range(8, 16)), list(range(16, FT))]

B_MIX, B_WO0, B_FI0, B_FO0, B_KV, B_QG, B_WO1, B_FI1, B_FO1 = 0, 32, 40, 84, 108, 125, 141, 149, 193
T_MIX, T_WO0, T_FI0, T_FO0, T_KV, T_QG, T_WO1, T_FI1, T_FO1 = 0, 32, 40, 84, 92, 109, 125, 133, 177
N_BLOCKS = 217

C_ID, C_MEAN, C_HEAD, C_PAIR, C_NEG, C_REP, C_SEQ, C_BLK, C_KEEP, C_KEEPC = 0, 128, 256, 384, 512, 640, 768, 776, 784, 1360
N_CONST = 1936
G_MIX, G_FFN, G_KV, G_ON, G_K, G_Q, G_BF, G_CW, G_CB = 0, 16, 32, 40, 41, 42, 43, 44, 44 + 2 * 3 * FT
N_GAIN = G_CB + 2 * FT


def tile_of(ap, i):
    if isinstance(i, int):
        return ap[:, i]
    return ap[:, bass.ds(i, 1)].rearrange("p a n -> p (a n)")


def row_of(ap, i):
    if isinstance(i, int):
        return ap[i]
    return ap[bass.ds(i, 1)].rearrange("a p n -> (a p) n")


def col_of(ap, i):
    return ap[:, bass.ds(i, 1)]


def wait(eng, sem, value):
    if isinstance(value, int) and value <= 0:
        return
    eng.wait_ge(sem, value)


def build(nc, d):
    ctx = ExitStack()
    with ctx:
        def sb(name, shape, dt=F32):
            return ctx.enter_context(nc.sbuf_tensor(name, shape, dt))

        def sem(name):
            return ctx.enter_context(nc.semaphore(name))

        h = sb("h", [P, DT, T])
        x_at = (nc.sbuf_base + 31) // 32 * 32
        xh = sb("xh", [P, DT, T], F32R)
        xl = sb("xl", [P, DT, T], F32R)
        w_raw = sb("w_raw", [P, RAW, 1024])
        w_hi = sb("w_hi", [P, SPL, 1024], F32R)
        w_lo = sb("w_lo", [P, SPL, 1024], F32R)
        ident = sb("ident", [P, P])
        mean_all = sb("mean_all", [P, P])
        gains = sb("gains", [P, N_GAIN])
        rms = sb("rms", [P, T])
        sq = sb("sq", [P, T])
        ssq = sb("ssq", [P, T])
        eps = sb("eps", [P, 1])
        base = (nc.sbuf_base + 63) // 64 * 64
        end = nc.sbuf_usable_end

        class Region:
            def __init__(self, tag, offset=base):
                self.tag, self.at = tag, offset

            def __call__(self, name, shape, dt=F32, size=4):
                n = size
                for s in shape[1:]:
                    n *= s
                t = nc.alloc_sbuf_tensor_at(f"{self.tag}_{name}", shape, dt, offset=self.at)
                self.at += (n + 63) // 64 * 64
                assert self.at <= end, (self.tag, name, self.at, end)
                return t

        mx = Region("mix")
        oh = mx("oh", [P, DT, T], F32R)
        ol = mx("ol", [P, DT, T], F32R)
        keep = mx("keep", [P, T])
        mean_head = mx("mean_head", [P, P])
        masks = mx("masks", [P, 8, P], U8, 1)
        blk = mx("blk", [P, 8])
        fr = mx("fr", [P, T]); fl = mx("fl", [P, T])
        qr = mx("qr", [P, T]); ql = mx("ql", [P, T])
        gr = mx("gr", [P, T]); gl = mx("gl", [P, T]); gate = mx("gate", [P, T])
        kd0 = fr
        b_ = mx("b", [P, 2, T]); k_ = mx("k", [P, 2, T]); q_ = mx("q", [P, 2, T])
        vT = mx("vT", [P, T])
        eb = mx("eb", [P, T]); qd = mx("qd", [P, T]); kd = mx("kd", [P, T])
        E = mx("E", [P, 2, T]); Z = mx("Z", [P, 2, T])
        A = mx("A", [P, NCH, P]); As = mx("As", [NS, NS])
        V = mx("V", [P, NCH, P]); Vs = mx("Vs", [NS, P]); Vb = mx("Vb", [NS, NSEQ, P])
        kT = mx("kT", [P, NCH, P]); kTs = mx("kTs", [NS, P])
        S = mx("S", [P, NCH, P])
        S0 = mx("S0", [P, NSEQ, P]); S1 = mx("S1", [P, NSEQ, P])
        orr = mx("orr", [P, T]); og = mx("og", [P, T])
        osq = og

        ff = Region("ffn")
        gh = ff("gh", [P, FT, T], F32R)
        glo = ff("glo", [P, FT, T], F32R)
        UW = 2 + SEQ + NSEQ * (2 + DSEQ)
        u = ff("u", [P, UW])
        a_ = ff("a", [P, T]); sil = ff("sil", [P, T])
        cst = ff("cst", [P, FT * 18])
        cin = ff("cin", [P, FT * 16])

        kv = Region("kv")
        x2h = kv("x2h", [P, DT, T], F32R)
        x2l = kv("x2l", [P, DT, T], F32R)
        KT = kv("KT", [P, DT, T])
        Vt = kv("Vt", [P, NCH, 8 * P])
        Vst = kv("Vst", [P, 8 * P])
        q_at = kv.at
        QT = kv("QT", [P, DT, T])
        GT = kv("GT", [P, DT, T])
        pair_mean = kv("pair_mean", [P, P])
        seq_col = kv("seq_col", [P, 8])
        gq = kv("gq", [P, 1])
        pg = kv("pg", [1, NSEQ * PAGES], I32)
        gate_log = kv("gate_log", [P, T])
        C = ssq
        t1 = Region("kvt", q_at)
        CL = t1("CL", [P, SEQ]); keep_c = t1("keep_c", [P, T])
        fx = t1("fx", [FOX, T]); fe = t1("fe", [FOX, T]); c16 = t1("c16", [FOX, T])
        rep16 = t1("rep16", [FOX, P])
        assert t1.at <= q_at + DT * T * 4
        t2 = Region("kvu", q_at + DT * T * 4)
        vT2 = t2("vT2", [P, 2, T])
        t3 = Region("dec", x_at)
        Kd = t3("Kd", [P, DT, T])
        Vd = t3("Vd", [P, PAGES, 8 * P])
        neg_rep = t3("neg_rep", [P, P])
        bfc = t3("bfc", [P, 2 * P + NSEQ * NS], BF16, 2)
        assert t3.at <= x_at + 2 * DT * T * 4
        t4 = Region("att")
        KX = t4("KX", [P, 2, SEQ]); QX = t4("QX", [P, 2, SEQ]); VX = t4("VX", [P, NCH, 2, P])
        Pr = t4("Pr", [P, 2, SEQ]); wide_at = t4.at; PT = t4("PT", [P, NCH, SEQ])
        Qb = t4("Qb", [P, 8 * 144]); Pd = t4("Pd", [P, T]); PTd = t4("PTd", [P, PAGES + 1, P])
        cc = t4("cc", [P, T])
        nm = t4("nm", [P, 8]); rs = t4("rs", [P, 8]); rr = t4("rr", [P, 8]); dm = t4("dm", [P, 4])
        assert t4.at <= base + 2 * DT * T * 4, t4.at - base
        t6 = Region("wide", wide_at)
        wide = t6("masks", [P, 2 * P + NSEQ * NS])
        t5 = Region("ao")
        ah = t5("ah", [P, DT, T], F32R); al = t5("al", [P, DT, T], F32R)

        acc = ctx.enter_context(nc.psum_tensor("acc", [P, 2, 2, 512], F32))
        aux = ctx.enter_context(nc.psum_tensor("aux", [P, 4, 512], F32))

        def S_ps(k):
            return acc[:, 0, k]
        T_ps, O_ps, D_ps, O2_ps = acc[:, 1, 0], acc[:, 1, 1], aux[:, 0:2], aux[:, 2:4]

        w_in = [sem(f"w_in{i}") for i in range(RAW)]
        hi_done, lo_done, block_done, evac = sem("hi_done"), sem("lo_done"), sem("block_done"), sem("evac")
        ld_const, ld_gain, ld_mask = sem("ld_const"), sem("ld_gain"), sem("ld_mask")
        ld_h = [sem(f"ld_h{i}") for i in range(DT)]
        x_hi, x_lo, sq_done, ssq_done = sem("x_hi"), sem("x_lo"), sem("sq_done"), sem("ssq_done")
        norm_ps, ln_done, rms_done = sem("norm_ps"), sem("ln_done"), sem("rms_done")
        setup = sem("setup")
        fr_ok, f_t, lf_ok, b_ok, kd0_ok, k_ok = [sem(n) for n in ("fr_ok", "f_t", "lf_ok", "b_ok", "kd0_ok", "k_ok")]
        qr_ok, q_t, ql_ok, q_sig, q_ok = [sem(n) for n in ("qr_ok", "q_t", "ql_ok", "q_sig", "q_ok")]
        gr_ok, g_t, gl_ok, g_sig, gate_ok = [sem(n) for n in ("gr_ok", "g_t", "gl_ok", "g_sig", "gate_ok")]
        vT_ok = sem("vT_ok")
        kdd_ok, kde_ok, eb_ok, kd_ok, qd_ok = [sem(n) for n in ("kdd_ok", "kde_ok", "eb_ok", "kd_ok", "qd_ok")]
        vT_ps, v_ok, vb_ok, kT_ps, kT_ok = [sem(n) for n in ("vT_ps", "v_ok", "vb_ok", "kT_ps", "kT_ok")]
        diff_ok, exp_ok, z_ok, gram_ps, gram_used = [sem(n) for n in ("diff_ok", "exp_ok", "z_ok", "gram_ps", "gram_used")]
        ds_ps, s_step, s_ok, o_ps, osq_ok, on_ps, oln_ok, orr_ok, og_ok, ogg_ok, oh_ok, ol_ok = [sem(n) for n in (
            "ds_ps", "s_step", "s_ok", "o_ps", "osq_ok", "on_ps", "oln_ok", "orr_ok", "og_ok", "ogg_ok", "oh_ok", "ol_ok")]
        s0_in, s0_mul, s1_ps, s1_ok, s1_out, s_out = [sem(n) for n in ("s0_in", "s0_mul", "s1_ps", "s1_ok", "s1_out", "s_out")]
        st_in, ubuf_ok, u_ok, c0_ok, c2_ok, sil_ok, silr_ok, prod_ok, gh_ok, glo_ok, cst_ok = [sem(n) for n in (
            "st_in", "ubuf_ok", "u_ok", "c0_ok", "c2_ok", "sil_ok", "silr_ok", "prod_ok", "gh_ok", "glo_ok", "cst_ok")]
        out_cst = sem("out_cst")
        h_ok, taking = sem("h_ok"), sem("taking")
        ld_kv, pg_in, cl_in, fx_ok, fb_ok, fe_t, flf_ok, c16_ok, f_out, c_scan, rep_ps, c_ok, c_dram = [sem(n) for n in (
            "ld_kv", "pg_in", "cl_in", "fx_ok", "fb_ok", "fe_t", "flf_ok", "c16_ok", "f_out", "c_scan", "rep_ps", "c_ok", "c_dram")]
        gq_ok, kr_ok, ksq_ok, km_ps, kln_ok, krk_ok, kn_ok, v2_ok, v2_ps, vt_ok, z_set = [sem(n) for n in (
            "gq_ok", "kr_ok", "ksq_ok", "km_ps", "kln_ok", "krk_ok", "kn_ok", "v2_ok", "v2_ps", "vt_ok", "z_set")]
        k_out, v_out = [sem("k_out0"), sem("k_out1")], [sem("v_out0"), sem("v_out1")]
        gx_ok, gx_t, gx_ls, gt_ok = [sem(n) for n in ("gx_ok", "gx_t", "gx_ls", "gt_ok")]
        cx_in, kx_ok, sc_ps, mx_ok, ex_ok, rc_ok, pn_ok, t_ps, pt_ok, pv_ps, go_ok = [sem(n) for n in (
            "cx_in", "kx_ok", "sc_ps", "mx_ok", "ex_ok", "rc_ok", "pn_ok", "t_ps", "pt_ok", "pv_ps", "go_ok")]
        kd_in, vd_in, kn_in, cc_ok, d_ps, dmx_ok, dex_ok, drc_ok, dpn_ok, dt_ps, dpt_ok, dpv_ps, dgo_ok, zero_ok = [
            sem(n) for n in ("kd_in", "vd_in", "kn_in", "cc_ok", "d_ps", "dmx_ok", "dex_ok", "drc_ok", "dpn_ok",
                             "dt_ps", "dpt_ok", "dpv_ps", "dgo_ok", "zero_ok")]
        ah_ok, al_ok, y_out = sem("ah_ok"), sem("al_ok"), sem("y_out")

        def halves(ap):
            return ap.rearrange("p (a n) -> p a n", a=2)

        def level(ap, m):
            w = T if m <= 4 else SEQ
            return ap[:, 0:w].rearrange("p (n two m) -> p n two m", two=2, m=m)

        block = ctx.enter_context(nc.Block())

        class Pos:
            def __init__(self, b0, i=0, step=0):
                assert step % RAW == 0
                self.b, self.slot, self.lap = b0 + step * i, b0 % RAW, b0 // RAW + (step // RAW) * i

        @block.sync
        def _(sp):
            sp.dma_start(h[:, 0, :], d["x"][0]).then_inc(ld_h[0], 16)
            sp.dma_start(gains[:], d["gains"]).then_inc(ld_gain, 16)

            def load(pos, src, width=1024):
                wait(sp, lo_done, pos.b - RAW + 1)
                sp.dma_start(w_raw[:, pos.slot, 0:width], src).then_inc(w_in[pos.slot], 16)

            def mixer(t, i0, i):
                for j in range(4):
                    load(Pos(B_MIX + 4 * i0 + j, i, 4), row_of(d["w_mix"], 4 * t + j))

            load(Pos(0), d["w_mix"][0])
            for m in range(1, DT):
                sp.dma_start(h[:, m, :], d["x"][m]).then_inc(ld_h[m], 16)
            sp.dma_start(ident[:], d["consts"][:, C_ID:C_ID + P]).then_inc(ld_const, 16)
            sp.dma_start(mean_all[:], d["consts"][:, C_MEAN:C_MEAN + P]).then_inc(ld_const, 16)
            sp.dma_start(mean_head[:], d["consts"][:, C_HEAD:C_HEAD + P]).then_inc(ld_const, 16)
            sp.dma_start(blk[:], d["consts"][:, C_BLK:C_BLK + 8]).then_inc(ld_const, 16)
            sp.dma_start(keep[:], d["consts"][:, C_KEEP:C_KEEP + T]).then_inc(ld_const, 16)
            sp.dma_start(Z[:].rearrange("p a n -> p (a n)")[:, 0:8 * P], d["masks"]).then_inc(ld_mask, 16)
            for j in range(1, 4):
                load(Pos(j), d["w_mix"][j])
            with sp.Fori(1, HEADS) as t:
                mixer(t, 0, t)

            def plain(b0, n, w):
                with sp.Fori(0, n // 4) as i:
                    for j in range(4):
                        load(Pos(b0 + j, i, 4), row_of(w, 4 * i + j))

            def ffn(layer, b_in, b_out):
                plain(b_in, 2 * FT, d[f"w_fi{layer}"])
                with sp.Fori(0, 2) as i:
                    for m in range(4):
                        for c, kts in enumerate(FO_K):
                            w = 128 * len(kts)
                            load(Pos(b_out + 3 * m + c, i, 12), row_of(d[f"w_fo{layer}"], 4 * i + m)[:, 1024 * c:1024 * c + w], w)

            plain(B_WO0, 8, d["w_o0"])
            ffn(0, B_FI0, B_FO0)
            for j in range(4):
                load(Pos(B_KV + j), d["w_kv"][j])
            sp.wait_ge(block_done, B_KV)
            sp.wait_ge(out_cst, 16)
            sp.dma_start(pg[:], d["pages"]).then_inc(pg_in, 16)
            for dst, src in ((pair_mean[:], d["consts"][:, C_PAIR:C_PAIR + P]),
                             (seq_col[:], d["consts"][:, C_SEQ:C_SEQ + 8]), (keep_c[:], d["consts"][:, C_KEEPC:C_KEEPC + T]),
                             (rep16[:], d["consts"][0:FOX, C_REP:C_REP + P])):
                sp.dma_start(dst, src).then_inc(ld_kv, 16)
            sp.wait_ge(pg_in, 16)
            n_phys = d["cache_f"].shape[0]

            def page(n, j):
                return sp.value_load(pg[0:1, bass.ds(PAGES * n + j, 1)], min_val=0, max_val=n_phys - 1)

            for n in range(NSEQ):
                for j in range(PAGES):
                    sp.dma_start(CL[FOX * n:FOX * n + FOX, P * j:P * j + P], row_of(d["cache_f"], page(n, j)))\
                        .then_inc(cl_in, 16)
            with sp.Fori(1, 4) as i:
                for j in range(4):
                    load(Pos(B_KV + j, i, 4), row_of(d["w_kv"], 4 * i + j))
            load(Pos(B_KV + 16), d["w_kv"][16])

            def pages(n):
                sp.wait_ge(pg_in, 16)
                wait(sp, d_ps, n)
                for j in range(PAGES):
                    sp.dma_start(Kd[:, :, P * j:P * j + P],
                                 row_of(d["cache_k"], page(n, j)).rearrange("p (a s) -> p a s", a=8)).then_inc(kd_in, 16)
                sp.wait_ge(pg_in, 16)
                wait(sp, dpv_ps, n)
                for j in range(PAGES):
                    sp.dma_start(Vd[:, j, :], row_of(d["cache_v"], page(n, j))).then_inc(vd_in, 16)

            for j in range(4):
                load(Pos(B_QG + j), d["w_qg"][j])
            with sp.Fori(1, 3) as i:
                for j in range(4):
                    load(Pos(B_QG + j, i, 4), row_of(d["w_qg"], 4 * i + j))
            sp.wait_ge(block_done, B_QG)
            sp.dma_start(neg_rep[:], d["consts"][:, C_NEG:C_NEG + P]).then_inc(ld_mask, 16)
            pages(0)
            for j in range(4):
                load(Pos(B_QG + 12 + j), d["w_qg"][12 + j])
            for j in range(4):
                load(Pos(B_WO1 + j), d["w_o1"][j])
            sp.wait_ge(block_done, B_WO1)
            sp.dma_start(wide[:], d["att_masks"]).then_inc(ld_mask, 16)
            with sp.Fori(1, NSEQ) as n:
                pages(n)
            for j in range(4, 8):
                load(Pos(B_WO1 + j), d["w_o1"][j])
            ffn(1, B_FI1, B_FO1)

        @block.scalar
        def _(act):
            def hi(pos, width=1024):
                wait(act, block_done, pos.b - SPL + 1)
                act.wait_ge(w_in[pos.slot], 16 * pos.lap + 16)
                nc.scalar.activation(w_hi[:, pos.slot % SPL, 0:width], w_raw[:, pos.slot, 0:width], ACT.Copy)\
                    .then_inc(hi_done, 1)

            def square(n, m):
                if m == 0:
                    wait(act, norm_ps, n // DT)
                    nc.scalar.activation(ssq[:], h[:, 0, :], ACT.Square).then_inc(sq_done, 1)
                else:
                    wait(act, ssq_done, n)
                    nc.scalar.activation(sq[:], tile_of(h, m), ACT.Square).then_inc(sq_done, 1)

            def gain_hi(dst, m, g):
                nc.scalar.activation(tile_of(dst, m), tile_of(h, m), ACT.Copy, scale=col_of(gains, g + m)).then_inc(x_hi, 1)

            def stats(n):
                act.wait_ge(norm_ps, n + 1)
                nc.scalar.activation(halves(sq[:]), aux[:, 0:2, 0:HALF], ACT.Ln, bias=eps[:, 0:1]).then_inc(ln_done, 1)
                act.wait_ge(ln_done, n + 1)
                nc.scalar.activation(rms[:], sq[:], ACT.Exp, scale=-0.5).then_inc(rms_done, 1)

            def softlog(src, dst, ready, done, n, *used):
                for s in used:
                    wait(act, s, n)
                act.wait_ge(ready, n + 1)
                nc.scalar.activation(dst[:], src[:], ACT.Abs).then_inc(done, 1)
                act.wait_ge(done, 3 * n + 1)
                nc.scalar.activation(dst[:], dst[:], ACT.Exp, scale=-1.0).then_inc(done, 1)
                act.wait_ge(done, 3 * n + 2)
                nc.scalar.activation(dst[:], dst[:], ACT.Ln, bias=1.0).then_inc(done, 1)

            def rec_exp(hd, j):
                w = T if LEVELS[j] <= 4 else SEQ
                act.wait_ge(diff_ok, 7 * hd + j + 1)
                nc.scalar.activation(E[:, j % 2, 0:w], E[:, j % 2, 0:w], ACT.Exp).then_inc(exp_ok, 1)

            def mixer(t, par, front, rec, split_next):
                hd, rp = t - 1, 1 - par
                b0 = 4 * t
                if front or split_next:
                    hi(Pos(1 if front else 0, t, 4))
                if rec:
                    softlog(gr, gl, gr_ok, g_t, hd, gate_ok)
                    act.wait_ge(b_ok, hd + 1)
                    wait(act, s_step, 4 * hd)
                    wait(act, s0_mul, hd)
                    nc.scalar.activation(eb[:], b_[:, rp, :], ACT.Exp).then_inc(eb_ok, 1)
                    act.wait_ge(kdd_ok, hd + 1)
                    nc.scalar.activation(kd[:], kd[:], ACT.Exp).then_inc(kde_ok, 1)
                    rec_exp(hd, 0)
                    act.wait_ge(vT_ps, hd + 1)
                    nc.scalar.activation(V[:], aux[:, 3, :].rearrange("p (c s) -> p c s", c=NCH), ACT.Copy).then_inc(v_ok, 1)
                    nc.scalar.activation(Vs[:], aux[0:NS, 2, 0:P], ACT.Copy).then_inc(v_ok, 1)
                    rec_exp(hd, 1)
                    act.wait_ge(kT_ps, hd + 1)
                    nc.scalar.activation(kT[:], aux[:, 3, :].rearrange("p (c s) -> p c s", c=NCH), ACT.Copy).then_inc(kT_ok, 1)
                    nc.scalar.activation(kTs[:], aux[0:NS, 2, 0:P], ACT.Copy).then_inc(kT_ok, 1)
                    act.wait_ge(gl_ok, hd + 1)
                    nc.scalar.activation(gl[:], gl[:], ACT.Exp).then_inc(g_sig, 1)
                if front:
                    hi(Pos(2, t, 4))
                if rec:
                    rec_exp(hd, 2)
                if front:
                    softlog(fr, fl, fr_ok, f_t, t, b_ok, kd0_ok)
                    hi(Pos(3, t, 4))
                if rec:
                    rec_exp(hd, 3)
                if front:
                    act.wait_ge(kd0_ok, t + 1)
                    nc.scalar.activation(k_[:, par, :], kd0[:], ACT.Exp).then_inc(k_ok, 1)
                if rec:
                    rec_exp(hd, 4)
                    rec_exp(hd, 5)
                if front:
                    softlog(qr, ql, qr_ok, q_t, t, q_ok)
                    hi(Pos(4, t, 4))
                    act.wait_ge(ql_ok, t + 1)
                    nc.scalar.activation(ql[:], ql[:], ACT.Exp).then_inc(q_sig, 1)
                if rec:
                    rec_exp(hd, 6)
                if rec:
                    act.wait_ge(o_ps, hd + 1)
                    wait(act, ol_ok, hd)
                    nc.scalar.activation(osq[:, 0:SEQ], aux[:, 0, :], ACT.Square).then_inc(osq_ok, 1)
                    nc.scalar.activation(osq[:, SEQ:T], aux[:, 1, 0:NS], ACT.Square).then_inc(osq_ok, 1)
                    act.wait_ge(on_ps, hd + 1)
                    nc.scalar.activation(orr[:, 0:SEQ], aux[:, 3, :], ACT.Ln, bias=eps[:, 0:1]).then_inc(oln_ok, 1)
                    nc.scalar.activation(orr[:, SEQ:T], aux[:, 1, 64:64 + NS], ACT.Ln, bias=eps[:, 0:1]).then_inc(oln_ok, 1)
                    act.wait_ge(oln_ok, 2 * hd + 2)
                    nc.scalar.activation(orr[:], orr[:], ACT.Exp, scale=-0.5).then_inc(orr_ok, 1)
                    act.wait_ge(ogg_ok, hd + 1)
                    nc.scalar.activation(tile_of(oh, hd), og[:], ACT.Copy).then_inc(oh_ok, 1)

            def out_tile(m, n_h, n_x, n_s, g):
                act.wait_ge(h_ok, n_h)
                square(n_s, m)
                if g is not None:
                    gain_hi(xh, m, g)

            nc.scalar.preload_act_table_set("natural_log_exp_and_others")
            act.wait_ge(setup, 1)
            act.wait_ge(ld_gain, 16)
            for m in range(DT):
                act.wait_ge(ld_h[m], 16)
                gain_hi(xh, m, G_MIX)
                if m == 0:
                    hi(Pos(0))
                square(m, m)
            hi(Pos(1))
            stats(0)
            def stage0():
                hi(Pos(2))
                softlog(fr, fl, fr_ok, f_t, 0)
                hi(Pos(3))
                act.wait_ge(kd0_ok, 1)
                nc.scalar.activation(k_[:, 0, :], kd0[:], ACT.Exp).then_inc(k_ok, 1)
                softlog(qr, ql, qr_ok, q_t, 0)
                hi(Pos(4))
                act.wait_ge(ql_ok, 1)
                nc.scalar.activation(ql[:], ql[:], ACT.Exp).then_inc(q_sig, 1)
            stage0()
            mixer(1, 1, True, True, True)
            with act.Fori(1, 4) as i:
                mixer(2 * i, 0, True, True, True)
                mixer(2 * i + 1, 1, True, True, True)
            mixer(8, 0, False, True, False)

            def ffn(layer, b_in, b_out, g_next, n_norm, h_base, s_base):
                n_h0 = h_base
                for m in range(DT):
                    hi(Pos(b_in - 8 + m + 1))
                    out_tile(m, n_h0 + m + 1, None, s_base + m, G_FFN + 8 * layer)
                hi(Pos(b_in + 1))
                stats(n_norm)
                nc.scalar.preload_act_table_set("silu_and_others")
                def pair(k, i, first):
                    f = 2 * i + k
                    n = FT * layer + f
                    if not first:
                        hi(Pos(b_in + 2 * k + 1, i, 4))
                    act.wait_ge(u_ok, n + 1)
                    cw = G_CW + 3 * FT * layer
                    for dst, src in ((a_[:, 0:SEQ], u[:, 2:2 + SEQ]),
                                     (a_[:, SEQ:T].rearrange("p (n t) -> p n t", n=NSEQ),
                                      u[:, 2 + SEQ:UW].rearrange("p (n t) -> p n t", n=NSEQ)[:, :, 2:])):
                        nc.scalar.activation(dst, src, ACT.Identity, scale=col_of(gains, cw + 2 * FT + f),
                                             bias=col_of(gains, G_CB + FT * layer + f)).then_inc(c0_ok, 1)
                    hi(Pos(b_in + 2 * k + 2, i, 4))
                    act.wait_ge(c2_ok, 2 * n + 2)
                    nc.scalar.activation(sil[:], a_[:], ACT.Silu).then_inc(sil_ok, 1)
                    act.wait_ge(prod_ok, n + 1)
                    nc.scalar.activation(tile_of(gh, f), sil[:], ACT.Copy).then_inc(gh_ok, 1)
                pair(0, 0, True)
                pair(1, 0, False)
                with act.Fori(1, FT // 2) as i:
                    pair(0, i, False)
                    pair(1, i, False)
                nc.scalar.preload_act_table_set("natural_log_exp_and_others")
                def body(i, last):
                    for m4 in range(4):
                        for c in range(3):
                            if not (last and m4 == 3 and c == 2):
                                nxt = (c + 1) % 3
                                hi(Pos(b_out + 3 * m4 + c + 1, i, 12), 128 * len(FO_K[nxt]) if not (m4 == 3 and c == 2) else 1024)
                        m = 4 * i + m4
                        act.wait_ge(h_ok, n_h0 + 8 + m + 1)
                        if g_next is not None:
                            if isinstance(i, int) and m == 0:
                                nc.scalar.activation(ssq[:], h[:, 0, :], ACT.Square).then_inc(sq_done, 1)
                            else:
                                act.wait_ge(ssq_done, s_base + 8 + m)
                                nc.scalar.activation(sq[:], tile_of(h, m), ACT.Square).then_inc(sq_done, 1)
                            gain_hi(xh, m, g_next)
                body(0, False)
                body(1, g_next is None)
            ffn(0, B_FI0, B_FO0, G_KV, 1, 0, 8)
            def key_norm(src, p, n):
                act.wait_ge(kr_ok, n + 1)
                nc.scalar.activation(sq[:], tile_of(src, p), ACT.Square).then_inc(ksq_ok, 1)
                act.wait_ge(km_ps, n + 1)
                nc.scalar.activation(halves(sq[:]), aux[:, 0:2, 0:HALF], ACT.Ln, bias=eps[:, 0:1]).then_inc(kln_ok, 1)
                wait(act, kn_ok, n)
                act.wait_ge(kln_ok, n + 1)
                nc.scalar.activation(sq[:], sq[:], ACT.Exp, scale=-0.5).then_inc(krk_ok, 1)

            def value_out(p, n):
                act.wait_ge(v2_ps, n + 1)
                nc.scalar.activation(Vt[:, :, bass.ds(P * p, P)], aux[:, 3, :].rearrange("p (c s) -> p c s", c=NCH), ACT.Copy)\
                    .then_inc(vt_ok, 1)
                nc.scalar.activation(Vst[0:NS, bass.ds(P * p, P)], aux[0:NS, 2, 0:P], ACT.Copy).then_inc(vt_ok, 1)

            hi(Pos(B_KV + 1))
            stats(2)
            act.wait_ge(fb_ok, 1)
            nc.scalar.activation(fe[:], fx[:], ACT.Abs).then_inc(fe_t, 1)
            act.wait_ge(fe_t, 1)
            nc.scalar.activation(fe[:], fe[:], ACT.Exp, scale=-1.0).then_inc(fe_t, 1)
            act.wait_ge(fe_t, 2)
            nc.scalar.activation(fe[:], fe[:], ACT.Ln, bias=1.0).then_inc(fe_t, 1)

            def kv_pair(k, p, i, step, first):
                hi(Pos(B_KV + 2 + 2 * k, i, step))
                if not first:
                    value_out(p - 1, p - 1)
                gain_hi(x2h, p, G_MIX + DT)
                hi(Pos(B_KV + 3 + 2 * k, i, step))
                key_norm(KT, p, p)
            kv_pair(0, 0, 0, 4, True)
            kv_pair(1, 1, 0, 4, False)
            with act.Fori(1, 4) as i:
                kv_pair(0, 2 * i, i, 4, False)
                kv_pair(1, 2 * i + 1, i, 4, False)

            def qg_pair(k, p, i, step, last_split):
                hi(Pos(B_QG + 1 + 2 * k, i, step))
                if isinstance(p, int) and p == 0:
                    value_out(7, 7)
                hi(Pos(B_QG + 2 + 2 * k, i, step))
                key_norm(QT, p, p + 8)
                g = tile_of(GT, p)
                act.wait_ge(gx_ok, p + 1)
                wait(act, gx_ls, p)
                nc.scalar.activation(gate_log[:], g, ACT.Abs).then_inc(gx_t, 1)
                act.wait_ge(gx_t, 3 * p + 1)
                nc.scalar.activation(gate_log[:], gate_log[:], ACT.Exp, scale=-1.0).then_inc(gx_t, 1)
                act.wait_ge(gx_t, 3 * p + 2)
                nc.scalar.activation(gate_log[:], gate_log[:], ACT.Ln, bias=1.0).then_inc(gx_t, 1)
                act.wait_ge(rms_done, 3)
                act.wait_ge(gx_ls, p + 1)
                nc.scalar.activation(g, g, ACT.Exp).then_inc(gt_ok, 1)
            qg_pair(0, 0, 0, 4, False)
            qg_pair(1, 1, 0, 4, False)
            with act.Fori(1, 4) as i:
                qg_pair(0, 2 * i, i, 4, False)
                qg_pair(1, 2 * i + 1, i, 4, False)

            def att(i):
                def ex(x):
                    n = 8 * i + x
                    w = P * (x % 4 + 1)
                    act.wait_ge(mx_ok, n + 1)
                    if not (isinstance(i, int) and x < 2):
                        act.wait_ge(t_ps, n - 1)
                        act.wait_ge(rc_ok, n - 1)
                    nc.scalar.activation(Pr[:, x % 2, 0:w], S_ps(x % 2)[:, 0:w], ACT.Exp, bias=nm[:, x:x + 1],
                                         accum_out=rs[:, x:x + 1]).then_inc(ex_ok, 1)

                def tcopy(x):
                    n = 8 * i + x
                    tb = x % 4
                    act.wait_ge(t_ps, n + 1)
                    if tb == 0 and not (isinstance(i, int) and x == 0):
                        act.wait_ge(pv_ps, 2 * i + x // 4)
                    nc.scalar.activation(PT[:, 0:tb + 1, P * tb:P * tb + P],
                                         T_ps[:, 0:P * (tb + 1)].rearrange("p (c s) -> p c s", c=tb + 1), ACT.Copy)\
                        .then_inc(pt_ok, 1)

                ex(0)
                ex(1)
                act.wait_ge(dmx_ok, i + 1)
                wait(act, dt_ps, i)
                nc.scalar.activation(halves(Pd[:]), D_ps[:, :, 0:HALF], ACT.Exp, bias=dm[:, 0:1],
                                     accum_out=dm[:, 1:2]).then_inc(dex_ok, 1)
                tcopy(0)
                ex(2)
                tcopy(1)
                ex(3)
                tcopy(2)
                ex(4)
                tcopy(3)
                ex(5)
                act.wait_ge(dt_ps, i + 1)
                wait(act, dpv_ps, i)
                nc.scalar.activation(PTd[:, 0:PAGES, :], D_ps[:, 0, :].rearrange("p (c s) -> p c s", c=PAGES), ACT.Copy)\
                    .then_inc(dpt_ok, 1)
                nc.scalar.activation(PTd[0:NS, PAGES, :], D_ps[0:NS, 1, 0:P], ACT.Copy).then_inc(dpt_ok, 1)
                tcopy(4)
                ex(6)
                tcopy(5)
                ex(7)
                tcopy(6)
                tcopy(7)
            att(0)
            with act.Fori(1, 8) as i:
                att(i)
            act.wait_ge(go_ok, 8)
            act.wait_ge(dgo_ok, 8)
            for p in range(DT):
                nc.scalar.activation(ah[:, p, :], GT[:, p, :], ACT.Copy).then_inc(ah_ok, 1)
            ffn(1, B_FI1, B_FO1, None, 3, 16, 24)

        @block.vector
        def _(dve):
            def lo(pos, width=1024):
                dve.wait_ge(hi_done, pos.b + 1)
                nc.vector.tensor_tensor(w_lo[:, pos.slot % SPL, 0:width], w_raw[:, pos.slot, 0:width],
                                        w_hi[:, pos.slot % SPL, 0:width].bitcast(F32), ALU.subtract).then_inc(lo_done, 1)

            def gain_lo(dst, src_hi, m, g, n):
                dve.wait_ge(x_hi, n + 1)
                nc.vector.scalar_tensor_tensor(out=tile_of(dst, m), in0=tile_of(h, m), scalar=col_of(gains, g + m),
                                               in1=tile_of(src_hi, m).bitcast(F32), op0=ALU.mult, op1=ALU.subtract)\
                    .then_inc(x_lo, 1)

            def scaled(dst, b, tp, done):
                dve.wait_ge(block_done, b + 1)
                nc.vector.tensor_tensor(halves(dst), acc[:, tp, :, 0:HALF], halves(rms[:]), ALU.mult).then_inc(done, 1)

            def logsig(x, l, ready, done, n):
                dve.wait_ge(ready, 3 * n + 3)
                nc.vector.scalar_tensor_tensor(out=l[:], in0=x[:], scalar=0.0, in1=l[:], op0=ALU.min, op1=ALU.subtract)\
                    .then_inc(done, 1)

            def diff(hd, rp, j):
                m = LEVELS[j]
                bv, ev = level(b_[:, rp], m), level(E[:, j % 2], m)
                mid = bv[:, :, 0, m - 1:m]
                n = bv.shape[1]
                wait(dve, z_ok, 7 * hd + j - 1)
                nc.vector.tensor_tensor(ev[:, :, 1, :], bv[:, :, 1, :], mid.to_broadcast([P, n, m]), ALU.subtract)
                nc.vector.tensor_tensor(ev[:, :, 0, :], mid.to_broadcast([P, n, m]), bv[:, :, 0, :], ALU.subtract)\
                    .then_inc(diff_ok, 1)

            def zed(hd, rp, j):
                m = LEVELS[j]
                kv, qv = level(k_[:, rp], m), level(q_[:, rp], m)
                ev, zv = level(E[:, j % 2], m), level(Z[:, j % 2], m)
                dve.wait_ge(exp_ok, 7 * hd + j + 1)
                nc.vector.tensor_tensor(zv[:, :, 1, :], qv[:, :, 1, :], ev[:, :, 1, :], ALU.mult)
                nc.vector.tensor_tensor(zv[:, :, 0, :], kv[:, :, 0, :], ev[:, :, 0, :], ALU.mult).then_inc(z_ok, 1)

            def take(hd, g):
                wait(dve, gram_used, 8 * hd + g)
                dve.wait_ge(gram_ps, 8 * hd + g + 1)
                nc.vector.sem_inc(taking, 1)
                mk = masks[:, g:g + 1, :]
                if g in SAMPLE_GRAM:
                    nc.vector.copy_predicated(As[:], masks[0:NS, SAMPLE_GRAM[g], 0:NS], aux[0:NS, 2, 0:NS])
                nc.vector.copy_predicated(A[:], mk.to_broadcast([P, NCH, P]),
                                          aux[:, g % 2, :].rearrange("p (c s) -> p c s", c=NCH)).then_inc(gram_used, 1)

            def mixer(t, par, front, rec):
                hd, rp = t - 1, 1 - par
                b0 = 4 * t
                if front:
                    lo(Pos(1, t, 4))
                if rec:
                    wait(dve, gate_ok, hd)
                    scaled(gr[:], b0 - 1, 1, gr_ok)
                    dve.wait_ge(gr_ok, hd + 1)
                    nc.vector.sem_inc(evac, 1)
                    pb = b_[:, rp, 0:SEQ].rearrange("p (c s) -> p c s", c=NCH)
                    sbv = b_[:, rp, SEQ:T].rearrange("p (c s) -> p c s", c=NSEQ)
                    wait(dve, kT_ps, hd)
                    nc.vector.tensor_tensor(kd[:, 0:SEQ].rearrange("p (c s) -> p c s", c=NCH),
                                            pb[:, :, CH - 1:CH].to_broadcast([P, NCH, CH]), pb, ALU.subtract)
                    nc.vector.tensor_tensor(kd[:, SEQ:T].rearrange("p (c s) -> p c s", c=NSEQ),
                                            sbv[:, :, DSEQ - 1:DSEQ].to_broadcast([P, NSEQ, DSEQ]), sbv, ALU.subtract)\
                        .then_inc(kdd_ok, 1)
                    diff(hd, rp, 0)
                    dve.wait_ge(q_ok, hd + 1)
                    dve.wait_ge(eb_ok, hd + 1)
                    nc.vector.tensor_tensor(qd[:], q_[:, rp], eb[:], ALU.mult).then_inc(qd_ok, 1)
                    dve.wait_ge(kde_ok, hd + 1)
                    nc.vector.tensor_tensor(kd[:], kd[:], k_[:, rp], ALU.mult).then_inc(kd_ok, 1)
                    logsig(gr, gl, g_t, gl_ok, hd)
                    diff(hd, rp, 1)
                    zed(hd, rp, 0)
                if front:
                    lo(Pos(2, t, 4))
                if rec:
                    take(hd, 0)
                if front:
                    wait(dve, k_ok, t)
                    scaled(fr[:], b0, 0, fr_ok)
                    dve.wait_ge(fr_ok, t + 1)
                    nc.vector.sem_inc(evac, 1)
                if rec:
                    diff(hd, rp, 2)
                    zed(hd, rp, 1)
                    take(hd, 1)
                if front:
                    logsig(fr, fl, f_t, lf_ok, t)
                    dve.wait_ge(lf_ok, t + 1)
                    nc.vector.tensor_tensor_scan(b_[:, par, :], keep[:], fl[:], 0.0, ALU.mult, ALU.add).then_inc(b_ok, 1)
                if front:
                    lo(Pos(3, t, 4))
                if rec:
                    diff(hd, rp, 3)
                    zed(hd, rp, 2)
                    take(hd, 2)
                if front:
                    wait(dve, q_ok, t)
                    scaled(qr[:], b0 + 1, 1, qr_ok)
                    dve.wait_ge(qr_ok, t + 1)
                    nc.vector.sem_inc(evac, 1)
                if rec:
                    diff(hd, rp, 4)
                    zed(hd, rp, 3)
                    take(hd, 3)
                    diff(hd, rp, 5)
                    zed(hd, rp, 4)
                    take(hd, 4)
                if front:
                    logsig(qr, ql, q_t, ql_ok, t)
                    lo(Pos(4, t, 4))
                if rec:
                    diff(hd, rp, 6)
                    zed(hd, rp, 5)
                    take(hd, 5)
                if front:
                    wait(dve, vT_ps, t)
                    scaled(vT[:], b0 + 2, 0, vT_ok)
                    dve.wait_ge(vT_ok, t + 1)
                    nc.vector.sem_inc(evac, 1)
                if rec:
                    zed(hd, rp, 6)
                    take(hd, 6)
                    take(hd, 7)
                    dve.wait_ge(ds_ps, hd + 1)
                    wait(dve, s_out, 16 * hd)
                    dv = aux[:, 3, :].rearrange("p (c v) -> p c v", c=NCH)
                    nc.vector.tensor_copy(S[:, 0], dv[:, 0]).then_inc(s_step, 1)
                    for c in range(1, NCH):
                        dve.wait_ge(s_step, 4 * hd + c)
                        nc.vector.scalar_tensor_tensor(out=S[:, c], in0=S[:, c - 1],
                                                       scalar=eb[:, CH * c + CH - 1:CH * c + CH],
                                                       in1=dv[:, c], op0=ALU.mult, op1=ALU.add).then_inc(s_step, 1)
                    dve.wait_ge(orr_ok, hd + 1)
                    g = gains[:, G_ON:G_ON + 1]
                    nc.vector.scalar_tensor_tensor(out=og[:, 0:SEQ], in0=aux[:, 0, :], scalar=g, in1=orr[:, 0:SEQ],
                                                   op0=ALU.mult, op1=ALU.mult).then_inc(og_ok, 1)
                    nc.vector.scalar_tensor_tensor(out=og[:, SEQ:T], in0=aux[:, 1, 0:NS], scalar=g, in1=orr[:, SEQ:T],
                                                   op0=ALU.mult, op1=ALU.mult).then_inc(og_ok, 1)
                    dve.wait_ge(og_ok, 2 * hd + 2)
                    dve.wait_ge(gate_ok, hd + 1)
                    nc.vector.tensor_tensor(og[:], og[:], gate[:], ALU.mult).then_inc(ogg_ok, 1)
                    for c in range(2):
                        dve.wait_ge(s1_ps, 2 * hd + c + 1)
                        dve.wait_ge(s0_mul, hd + 1)
                        s1 = S1[:, 4 * c:4 * c + 4]
                        nc.vector.tensor_tensor(s1, s1, aux[:, 2, :].rearrange("p (n v) -> p n v", n=4), ALU.add)\
                            .then_inc(s1_ok, 1)
                    dve.wait_ge(oh_ok, hd + 1)
                    nc.vector.tensor_tensor(tile_of(ol, hd), og[:], tile_of(oh, hd).bitcast(F32), ALU.subtract)\
                        .then_inc(ol_ok, 1)

            nc.vector.memset(eps[:], EPS).then_inc(setup, 1)
            nc.vector.memset(A[:], 0.0)
            nc.vector.memset(As[:], 0.0)
            dve.wait_ge(ld_gain, 16)
            for m in range(DT):
                gain_lo(xl, xh, m, G_MIX, m)
                if m == 0:
                    lo(Pos(0))
            dve.wait_ge(rms_done, 1)
            dve.wait_ge(ld_const, 80)
            dve.wait_ge(ld_mask, 16)
            nc.vector.tensor_copy(masks[:].rearrange("p a n -> p (a n)"), Z[:].rearrange("p a n -> p (a n)")[:, 0:8 * P])\
                .then_inc(setup, 1)
            dve.wait_ge(setup, 2)
            mixer(0, 0, True, False)
            mixer(1, 1, True, True)
            with dve.Fori(1, 4) as i:
                mixer(2 * i, 0, True, True)
                mixer(2 * i + 1, 1, True, True)
            mixer(8, 0, False, True)

            def add_h(m, b, tp, n_h):
                dve.wait_ge(block_done, b + 1)
                nc.vector.tensor_tensor(halves(tile_of(h, m)), halves(tile_of(h, m)), acc[:, tp, :, 0:HALF], ALU.add)\
                    .then_inc(h_ok, 1)
                dve.wait_ge(h_ok, n_h)
                nc.vector.sem_inc(evac, 1)

            def ffn(layer, b_in, b_out, g_next, n_norm, h_base, x_base, t_in, t_out):
                for m in range(DT):
                    lo(Pos(b_in - 8 + m + 1))
                    add_h(m, b_in - 8 + m, (t_in - 8 + m) % 2, h_base + m + 1)
                    gain_lo(xl, xh, m, G_FFN + 8 * layer, x_base + m)
                lo(Pos(b_in + 1))
                dve.wait_ge(rms_done, n_norm + 1)
                dve.wait_ge(s_out, 16 * HEADS)
                dve.wait_ge(s1_out, 16 * HEADS)
                nc.vector.memset(u[:, 0:2], 0.0)
                def pair(k, i, first):
                    f = 2 * i + k
                    n = FT * layer + f
                    b = b_in + 2 * f
                    if not first:
                        lo(Pos(b_in + 2 * k + 1, i, 4))
                    tp = (t_in) % 2
                    dve.wait_ge(block_done, b + 1)
                    wait(dve, cst_ok, 2 * n)
                    wait(dve, c2_ok, 2 * n)
                    nc.vector.tensor_tensor(u[:, 2:2 + HALF], acc[:, tp, 0, 0:HALF], rms[:, 0:HALF], ALU.mult)
                    nc.vector.tensor_tensor(u[:, 2 + HALF:2 + SEQ], acc[:, tp, 1, 0:SEQ - HALF], rms[:, HALF:SEQ], ALU.mult)
                    us = u[:, 2 + SEQ:UW].rearrange("p (n t) -> p n t", n=NSEQ)
                    nc.vector.tensor_tensor(us[:, :, 2:], acc[:, tp, 1, SEQ - HALF:HALF].rearrange("p (n t) -> p n t", n=NSEQ),
                                            rms[:, SEQ:T].rearrange("p (n t) -> p n t", n=NSEQ), ALU.mult).then_inc(u_ok, 1)
                    dve.wait_ge(u_ok, n + 1)
                    nc.vector.sem_inc(evac, 1)
                    lo(Pos(b_in + 2 * k + 2, i, 4))
                    cw = G_CW + 3 * FT * layer
                    dve.wait_ge(c0_ok, 2 * n + 2)
                    dve.wait_ge(ubuf_ok, n + 1)
                    at = a_[:, SEQ:T].rearrange("p (n t) -> p n t", n=NSEQ)
                    for j in (1, 0):
                        w = col_of(gains, cw + FT * j + f)
                        nc.vector.scalar_tensor_tensor(out=a_[:, 0:SEQ], in0=u[:, j:j + SEQ], scalar=w, in1=a_[:, 0:SEQ],
                                                       op0=ALU.mult, op1=ALU.add)
                        nc.vector.scalar_tensor_tensor(out=at, in0=us[:, :, j:j + DSEQ], scalar=w, in1=at,
                                                       op0=ALU.mult, op1=ALU.add).then_inc(c2_ok, 1)
                        if j == 1:
                            dve.wait_ge(c2_ok, 2 * n + 1)
                    dve.wait_ge(silr_ok, n + 1)
                    dve.wait_ge(block_done, b + 2)
                    nc.vector.tensor_tensor(halves(sil[:]), acc[:, 1 - tp, :, 0:HALF], halves(sil[:]), ALU.mult).then_inc(prod_ok, 1)
                    dve.wait_ge(prod_ok, n + 1)
                    nc.vector.sem_inc(evac, 1)
                    dve.wait_ge(gh_ok, n + 1)
                    nc.vector.tensor_tensor(tile_of(glo, f), sil[:], tile_of(gh, f).bitcast(F32), ALU.subtract).then_inc(glo_ok, 1)
                pair(0, 0, True)
                pair(1, 0, False)
                with dve.Fori(1, FT // 2) as i:
                    pair(0, i, False)
                    pair(1, i, False)
                def body(i, last):
                    for m4 in range(4):
                        for c in range(3):
                            if not (last and m4 == 3 and c == 2):
                                nxt = (c + 1) % 3
                                lo(Pos(b_out + 3 * m4 + c + 1, i, 12), 128 * len(FO_K[nxt]) if not (m4 == 3 and c == 2) else 1024)
                        m = 4 * i + m4
                        add_h(m, b_out + 3 * m + 2, (t_out + m4) % 2, h_base + 8 + m + 1)
                        if g_next is not None:
                            gain_lo(xl, xh, m, g_next, x_base + 8 + m)
                body(0, False)
                body(1, g_next is None)
            ffn(0, B_FI0, B_FO0, G_KV, 1, 0, 8, T_FI0, T_FO0)
            def key_raw(dst, p, n, b, tp):
                scaled(tile_of(dst, p), b, tp, kr_ok)
                dve.wait_ge(kr_ok, n + 1)
                nc.vector.sem_inc(evac, 1)

            def key_gain(dst, p, n, g):
                dve.wait_ge(krk_ok, n + 1)
                nc.vector.scalar_tensor_tensor(out=tile_of(dst, p), in0=tile_of(dst, p), scalar=g, in1=sq[:],
                                               op0=ALU.mult, op1=ALU.mult).then_inc(kn_ok, 1)

            lo(Pos(B_KV + 1))
            dve.wait_ge(rms_done, 3)
            dve.wait_ge(block_done, B_KV + 1)
            dve.wait_ge(ld_kv, 64)
            nc.vector.tensor_scalar(gq[:], gains[:, G_Q:G_Q + 1], 0.125, None, ALU.mult).then_inc(gq_ok, 1)
            nc.vector.memset(Vst[:], 0.0).then_inc(z_set, 1)
            nc.vector.tensor_tensor(halves(fx[:]), acc[0:FOX, T_KV % 2, :, 0:HALF], halves(rms[0:FOX, :]), ALU.mult).then_inc(fx_ok, 1)
            dve.wait_ge(fx_ok, 1)
            nc.vector.sem_inc(evac, 1)
            nc.vector.tensor_scalar(fx[:], fx[:], gains[0:FOX, G_BF:G_BF + 1], None, ALU.add).then_inc(fb_ok, 1)
            lo(Pos(B_KV + 2))
            dve.wait_ge(fe_t, 3)
            nc.vector.scalar_tensor_tensor(out=fx[:], in0=fx[:], scalar=0.0, in1=fe[:], op0=ALU.min, op1=ALU.subtract)\
                .then_inc(flf_ok, 1)
            dve.wait_ge(flf_ok, 1)
            nc.vector.tensor_tensor_scan(c16[:], keep_c[0:FOX, :], fx[:], 0.0, ALU.mult, ALU.add).then_inc(c16_ok, 1)
            dve.wait_ge(cl_in, 16 * NSEQ * PAGES)
            nc.vector.tensor_tensor_scan(C[:, 0:SEQ], keep_c[:, 0:SEQ], CL[:], 0.0, ALU.mult, ALU.add).then_inc(c_scan, 1)
            dve.wait_ge(c_scan, 1)
            dve.wait_ge(rep_ps, 1)
            nc.vector.tensor_scalar(C[:, SEQ:T], aux[:, 2, 0:NS], C[:, SEQ - 1:SEQ], None, ALU.add).then_inc(c_ok, 1)

            def kv_pair(k, p, i, step, first):
                b = B_KV + 1 + 2 * p
                if not first:
                    lo(Pos(B_KV + 2 + 2 * k, i, step))
                key_raw(KT, p, p, b, (T_KV + 1) % 2)
                gain_lo(x2l, x2h, p, G_MIX + DT, 24 + p)
                lo(Pos(B_KV + 3 + 2 * k, i, step))
                if not (isinstance(p, int) and p < 2):
                    dve.wait_ge(v_out[k], 16 * (i if k == 0 else i))
                scaled(vT2[:, k, :], b + 1, T_KV % 2, v2_ok)
                dve.wait_ge(v2_ok, p + 1)
                nc.vector.sem_inc(evac, 1)
                key_gain(KT, p, p, gains[:, G_K:G_K + 1])
            kv_pair(0, 0, 0, 4, True)
            kv_pair(1, 1, 0, 4, False)
            with dve.Fori(1, 4) as i:
                kv_pair(0, 2 * i, i, 4, False)
                kv_pair(1, 2 * i + 1, i, 4, False)
            dve.wait_ge(gq_ok, 1)

            def qg_pair(k, p, i, step):
                b = B_QG + 2 * p
                lo(Pos(B_QG + 1 + 2 * k, i, step))
                if isinstance(p, int) and p == 0:
                    dve.wait_ge(c_dram, 16)
                    dve.wait_ge(v_out[0], 64)
                    dve.wait_ge(v_out[1], 64)
                    dve.wait_ge(f_out, 16)
                    dve.wait_ge(v2_ps, 8)
                    dve.wait_ge(c_ok, 1)
                key_raw(QT, p, p + 8, b, T_QG % 2)
                lo(Pos(B_QG + 2 + 2 * k, i, step))
                scaled(tile_of(GT, p), b + 1, (T_QG + 1) % 2, gx_ok)
                dve.wait_ge(gx_ok, p + 1)
                nc.vector.sem_inc(evac, 1)
                key_gain(QT, p, p + 8, gq[:, 0:1])
                dve.wait_ge(gx_t, 3 * p + 3)
                g = tile_of(GT, p)
                nc.vector.scalar_tensor_tensor(out=g, in0=g, scalar=0.0, in1=gate_log[:], op0=ALU.min, op1=ALU.subtract)\
                    .then_inc(gx_ls, 1)
            qg_pair(0, 0, 0, 4)
            qg_pair(1, 1, 0, 4)
            with dve.Fori(1, 4) as i:
                qg_pair(0, 2 * i, i, 4)
                qg_pair(1, 2 * i + 1, i, 4)

            def att(i):
                def mx(x):
                    n = 8 * i + x
                    w = P * (x % 4 + 1)
                    dve.wait_ge(sc_ps, n + 1)
                    if not isinstance(i, int):
                        dve.wait_ge(ex_ok, n - 7)
                    nc.vector.tensor_reduce(nm[:, x:x + 1], S_ps(x % 2)[:, 0:w], AX.X, ALU.max, negate=True).then_inc(mx_ok, 1)

                def norm(x):
                    n = 8 * i + x
                    w = P * (x % 4 + 1)
                    dve.wait_ge(ex_ok, n + 1)
                    nc.vector.reciprocal(rr[:, x:x + 1], rs[:, x:x + 1]).then_inc(rc_ok, 1)
                    dve.wait_ge(rc_ok, n + 1)
                    nc.vector.tensor_scalar(Pr[:, x % 2, 0:w], Pr[:, x % 2, 0:w], rr[:, x:x + 1], None, ALU.mult).then_inc(pn_ok, 1)

                wait(dve, d_ps, i)
                nc.vector.tensor_scalar(cc[:], C[:], col_of(seq_col, i), None, ALU.mult).then_inc(cc_ok, 1)
                mx(0)
                mx(1)
                norm(0)
                dve.wait_ge(d_ps, i + 1)
                nc.vector.tensor_reduce(dm[:, 0:1], D_ps[:, :, 0:HALF], AX.XY, ALU.max, negate=True).then_inc(dmx_ok, 1)
                norm(1)
                mx(2)
                dve.wait_ge(dex_ok, i + 1)
                nc.vector.reciprocal(dm[:, 2:3], dm[:, 1:2]).then_inc(drc_ok, 1)
                dve.wait_ge(drc_ok, i + 1)
                nc.vector.tensor_scalar(Pd[:], Pd[:], dm[:, 2:3], None, ALU.mult).then_inc(dpn_ok, 1)
                mx(3)
                norm(2)
                mx(4)
                norm(3)
                mx(5)
                norm(4)
                mx(6)
                norm(5)
                mx(7)
                norm(6)
                norm(7)
                dve.wait_ge(dpv_ps, i + 1)
                for a in range(2):
                    r = slice(64 * a, 64 * a + 64)
                    flat = O2_ps[r, :, :].rearrange("p a n -> p (a n)")
                    g = GT[r, :, bass.ds(SEQ + DSEQ * i, DSEQ)]
                    nc.vector.tensor_tensor(g[:, 0:7, :], flat[:, 0:7 * 144].rearrange("p (k c) -> p k c", c=144)[:, :, 8 * a:8 * a + 8],
                                            g[:, 0:7, :], ALU.mult)
                    last = nc.vector.tensor_tensor(g[:, 7, :], flat[:, 7 * 144 + 8 * a:7 * 144 + 8 * a + 8], g[:, 7, :], ALU.mult)
                last.then_inc(dgo_ok, 1)
                dve.wait_ge(pv_ps, 2 * i + 2)
                g = tile_of(GT, i)[:, 0:SEQ]
                nc.vector.tensor_tensor(g, O_ps[:, :], g, ALU.mult).then_inc(go_ok, 1)
            dve.wait_ge(block_done, B_WO1)
            nc.vector.memset(dm[:], 0.0).then_inc(zero_ok, 1)
            dve.wait_ge(ld_mask, 48)
            nc.vector.tensor_copy(bfc[:], wide[:]).then_inc(zero_ok, 1)
            dve.wait_ge(gt_ok, 8)
            att(0)
            with dve.Fori(1, 8) as i:
                att(i)
            for p in range(DT):
                dve.wait_ge(ah_ok, p + 1)
                nc.vector.tensor_tensor(al[:, p, :], GT[:, p, :], ah[:, p, :].bitcast(F32), ALU.subtract).then_inc(al_ok, 1)
            ffn(1, B_FI1, B_FO1, None, 3, 16, 32, T_FI1, T_FO1)

        @block.gpsimd
        def _(pool):
            def add_square(n):
                pool.wait_ge(sq_done, n + 1)
                nc.gpsimd.tensor_tensor(ssq[:], ssq[:], sq[:], ALU.add).then_inc(ssq_done, 1)

            def first_square(n):
                pool.wait_ge(sq_done, n + 1)
                nc.gpsimd.sem_inc(ssq_done, 1)

            first_square(0)
            for m in range(1, DT):
                if m > 1:
                    pool.wait_ge(ssq_done, m)
                add_square(m)

            def mixer(t, par, front, rec):
                hd, rp = t - 1, 1 - par
                if rec:
                    pool.wait_ge(s0_in, 16 * hd + 16)
                    pool.wait_ge(eb_ok, hd + 1)
                    wait(pool, s1_out, 16 * hd)
                    e = eb[:, SEQ:T].rearrange("p (n t) -> p n t", n=NSEQ)[:, :, DSEQ - 1:DSEQ]
                    nc.gpsimd.tensor_tensor(S1[:], S0[:], e.to_broadcast([P, NSEQ, P]), ALU.mult).then_inc(s0_mul, 1)
                    pool.wait_ge(v_ok, 2 * hd + 2)
                    wait(pool, s1_ps, 2 * hd)
                    nc.gpsimd.tensor_tensor(Vb[:], Vs[:].unsqueeze(1).to_broadcast([NS, NSEQ, P]),
                                            blk[0:NS, :].unsqueeze(2).to_broadcast([NS, NSEQ, P]), ALU.mult).then_inc(vb_ok, 1)
                    pool.wait_ge(g_sig, hd + 1)
                    wait(pool, ogg_ok, hd)
                    nc.gpsimd.tensor_tensor(gate[:], gr[:], gl[:], ALU.mult).then_inc(gate_ok, 1)
                if front:
                    pool.wait_ge(lf_ok, t + 1)
                    nc.gpsimd.tensor_tensor(kd0[:], fl[:], fr[:], ALU.subtract).then_inc(kd0_ok, 1)
                    pool.wait_ge(q_sig, t + 1)
                    nc.gpsimd.tensor_tensor(q_[:, par], qr[:], ql[:], ALU.mult).then_inc(q_ok, 1)
                if rec and front:
                    pool.wait_ge(o_ps, hd + 1)
                    pool.dma_start(S0[:].rearrange("p n v -> p (n v)"), row_of(d["s0"], t)).then_inc(s0_in, 16)
                if rec:
                    pool.wait_ge(s_step, 4 * hd + 4)
                    pool.dma_start(row_of(d["hgrn_p"], hd), S[:, NCH - 1]).then_inc(s_out, 16)
                    pool.wait_ge(ld_const, 80)
                    pool.wait_ge(s1_ok, 2 * hd + 2)
                    pool.dma_start(row_of(d["hgrn_s"], hd), S1[:].rearrange("p n v -> p (n v)")).then_inc(s1_out, 16)
            pool.dma_start(S0[:].rearrange("p n v -> p (n v)"), d["s0"][0]).then_inc(s0_in, 16)
            pool.wait_ge(ld_const, 80)
            mixer(0, 0, True, False)
            mixer(1, 1, True, True)
            with pool.Fori(1, 4) as i:
                mixer(2 * i, 0, True, True)
                mixer(2 * i + 1, 1, True, True)
            mixer(8, 0, False, True)

            def squares(s_base):
                first_square(s_base)
                pool.wait_ge(ssq_done, s_base + 1)
                add_square(s_base + 1)
                with pool.Fori(2, DT) as m:
                    pool.wait_ge(ssq_done, s_base + m)
                    add_square(s_base + m)

            def ffn(layer, b_in, has_next, s_base):
                squares(s_base)
                pool.wait_ge(x_lo, s_base + 8 * layer + 8)
                pool.wait_ge(s_out, 16 * HEADS)
                pool.wait_ge(s1_out, 16 * HEADS)
                wait(pool, out_cst, 16 * layer)
                pool.dma_start(cin[:], d["conv_in"][layer]).then_inc(st_in, 16)
                pool.wait_ge(st_in, 16 * layer + 16)
                def pair(f):
                    n = FT * layer + f
                    us = u[:, 2 + SEQ:UW].rearrange("p (n t) -> p n t", n=NSEQ)
                    ci = cin[:, bass.ds(16 * f, 16)].rearrange("p (n t) -> p n t", n=NSEQ)
                    wait(pool, c2_ok, 2 * n)
                    nc.gpsimd.tensor_copy(us[:, :, 0:2], ci).then_inc(ubuf_ok, 1)
                    pool.wait_ge(u_ok, n + 1)
                    nc.gpsimd.tensor_copy(cst[:, bass.ds(18 * f, 2)], u[:, SEQ:SEQ + 2]).then_inc(cst_ok, 1)
                    nc.gpsimd.tensor_copy(cst[:, bass.ds(18 * f + 2, 16)].rearrange("p (n t) -> p n t", n=NSEQ),
                                          us[:, :, DSEQ:DSEQ + 2]).then_inc(cst_ok, 1)
                    pool.wait_ge(sil_ok, n + 1)
                    nc.gpsimd.tensor_tensor(sil[:], sil[:], rms[:], ALU.mult).then_inc(silr_ok, 1)
                pair(0)
                with pool.Fori(1, FT) as f:
                    pair(f)
                pool.wait_ge(cst_ok, 2 * FT * (layer + 1))
                pool.dma_start(d["conv_out"][layer], cst[:]).then_inc(out_cst, 16)
                if has_next:
                    squares(s_base + 8)
            ffn(0, B_FI0, True, 8)
            pool.wait_ge(flf_ok, 1)
            pool.dma_start(d["f_out"], fx[:]).then_inc(f_out, 16)
            pool.wait_ge(c16_ok, 1)
            pool.dma_start(d["c_row"], c16[:]).then_inc(c_dram, 16)

            def kv_pair(k, p):
                pool.wait_ge(v2_ok, p + 1)
                pool.dma_start(row_of(d["v_out"], p), vT2[:, k, :]).then_inc(v_out[k], 16)
                pool.wait_ge(kn_ok, p + 1)
                pool.dma_start(row_of(d["k_out"], p), tile_of(KT, p)).then_inc(k_out[k], 16)
            with pool.Fori(0, 4) as i:
                kv_pair(0, 2 * i)
                kv_pair(1, 2 * i + 1)

            pool.wait_ge(block_done, B_WO1)
            pool.wait_ge(c_dram, 16)
            for z in (KX, QX, VX, Qb, PTd):
                nc.gpsimd.memset(z[:], 0.0).then_inc(zero_ok, 1)
            pool.wait_ge(zero_ok, 7)
            nc.gpsimd.memset(QX[64:65, 0, :], -1.0).then_inc(zero_ok, 1)
            pool.wait_ge(zero_ok, 8)
            nc.gpsimd.memset(QX[0:1, 1, :], -1.0).then_inc(zero_ok, 1)
            pool.wait_ge(zero_ok, 9)
            nc.gpsimd.tensor_copy(Kd[:, :, SEQ:T], KT[:, :, SEQ:T]).then_inc(kn_in, 1)
            pool.wait_ge(kn_in, 1)

            def att(i):
                if not isinstance(i, int):
                    pool.wait_ge(sc_ps, 8 * i)
                    pool.wait_ge(pv_ps, 2 * i)
                    pool.wait_ge(kx_ok, 8 * i)
                for a in range(2):
                    r, o = slice(64 * a, 64 * a + 64), 64 * (1 - a)
                    row = d["c_row"][bass.ds(2 * i + a, 1), 0:SEQ]
                    pool.dma_start(KX[o:o + 1, a, :], row).then_inc(cx_in, 16)
                    for j, (dst, src) in enumerate((
                            (KX[r, a, :], KT[r, bass.ds(i, 1), 0:SEQ].rearrange("p a n -> p (a n)")),
                            (QX[r, a, :], QT[r, bass.ds(i, 1), 0:SEQ].rearrange("p a n -> p (a n)")),
                            (VX[:, :, a, 64 * a:64 * a + 64], Vt[:, :, bass.ds(P * i + 64 * a, 64)]),
                            (Qb[r, :].rearrange("p (k c) -> p k c", c=144)[:, :, 8 * a:8 * a + 8],
                             QT[r, :, bass.ds(SEQ + DSEQ * i, DSEQ)]))):
                        n = 8 * i + 4 * a + j
                        if j == 3:
                            wait(pool, d_ps, i)
                        wait(pool, kx_ok, n)
                        nc.gpsimd.tensor_copy(dst, src).then_inc(kx_ok, 1)
            att(0)
            with pool.Fori(1, 8) as i:
                att(i)
            ffn(1, B_FI1, False, 24)
            for m in range(DT):
                pool.wait_ge(h_ok, 24 + m + 1)
                pool.dma_start(d["y"][m], h[:, m, :]).then_inc(y_out, 16)
            pool.wait_ge(y_out, 16 * DT)
            pool.wait_ge(out_cst, 32)
            pool.wait_ge(f_out, 16)
            for k in range(2):
                pool.wait_ge(k_out[k], 64)
                pool.wait_ge(v_out[k], 64)

        @block.tensor
        def _(pe):
            def gemm(pos, tile, tp, kts, rh, rl, first=True, last=True, wait_x=None, mid=None):
                pe.wait_ge(lo_done, pos.b + 1)
                if first:
                    wait(pe, evac, tile - 1)
                sp_ = pos.slot % SPL
                for j, kt in enumerate(kts):
                    if wait_x is not None:
                        pe.wait_ge(wait_x[0], wait_x[1] + kt + 1)
                    for n, (W, X) in enumerate(((w_hi, rl), (w_lo, rh), (w_hi, rh))):
                        for hf in range(2):
                            mm = nc.tensor.matmul(acc[:, tp, hf, 0:HALF], W[:, sp_, 128 * j:128 * j + 128],
                                                  X[:, kt, HALF * hf:HALF * hf + HALF],
                                                  start=(first and j == 0 and n == 0),
                                                  stop=(last and j == len(kts) - 1 and n == 2))
                    if mid is not None and j == 3:
                        mid()
                mm.then_inc(block_done, 1)

            def norm(n, n_ssq):
                pe.wait_ge(ssq_done, n_ssq)
                for hf in range(2):
                    mm = nc.tensor.matmul(aux[:, hf, 0:HALF], mean_all[:], ssq[:, HALF * hf:HALF * hf + HALF],
                                          start=True, stop=True)
                mm.then_inc(norm_ps, 1)

            def gram(hd, rp, g):
                if g == 0:
                    pe.wait_ge(k_ok, hd + 1)
                    pe.wait_ge(q_ok, hd + 1)
                    lhs, rhs = k_[:, rp], q_[:, rp]
                else:
                    pe.wait_ge(z_ok, 7 * hd + g)
                    lhs = rhs = Z[:, (g - 1) % 2]
                wait(pe, gram_used, 8 * hd + g - 1)
                for c in range(NCH):
                    mm = nc.tensor.matmul(aux[:, g % 2, CH * c:CH * c + CH], lhs[:, CH * c:CH * c + CH],
                                          rhs[:, CH * c:CH * c + CH], start=True, stop=True)
                if g in SAMPLE_GRAM:
                    if g == 3:
                        pe.wait_ge(kT_ok, 2 * hd + 2)
                        lhs, rhs = k_[:, rp], q_[:, rp]
                    else:
                        pe.wait_ge(gram_used, 8 * hd + g)
                    mm = nc.tensor.matmul(aux[0:NS, 2, 0:NS], lhs[:, SEQ:T], rhs[:, SEQ:T], start=True, stop=True)
                mm.then_inc(gram_ps, 1)

            def turn(src):
                for c in range(NCH):
                    nc.tensor.transpose(aux[:, 3, CH * c:CH * c + CH], src[:, CH * c:CH * c + CH], ident[:])
                return nc.tensor.transpose(aux[0:NS, 2, 0:P], src[:, SEQ:T], ident[:])

            def mixer(t, par, front, rec):
                hd, rp = t - 1, 1 - par
                b0 = 4 * t

                def q0():
                    pe.wait_ge(vT_ok, hd + 1)
                    wait(pe, orr_ok, hd)
                    wait(pe, s1_ok, 2 * hd)
                    turn(vT).then_inc(vT_ps, 1)
                    wait(pe, og_ok, 2 * hd)
                    gram(hd, rp, 0)

                def q0b():
                    pe.wait_ge(kd_ok, hd + 1)
                    pe.wait_ge(v_ok, 2 * hd + 2)
                    turn(kd).then_inc(kT_ps, 1)
                    gram(hd, rp, 1)

                def ds():
                    pe.wait_ge(kT_ok, 2 * hd + 2)
                    for c in range(NCH):
                        mm = nc.tensor.matmul(aux[:, 3, CH * c:CH * c + CH], kT[:, c], V[:, c], start=True, stop=True)
                    mm.then_inc(ds_ps, 1)

                def outs():
                    pe.wait_ge(gram_used, 8 * hd + 8)
                    pe.wait_ge(s_step, 4 * hd + 3)
                    pe.wait_ge(s0_in, 16 * hd + 16)
                    pe.wait_ge(qd_ok, hd + 1)
                    for c in range(NCH):
                        o = aux[:, 0, CH * c:CH * c + CH]
                        nc.tensor.matmul(o, V[:, c], A[:, c], start=True, stop=(c == 0))
                        if c:
                            nc.tensor.matmul(o, S[:, c - 1], qd[:, CH * c:CH * c + CH], start=False, stop=True)
                    o = aux[:, 1, 0:NS]
                    for n in range(NSEQ):
                        nc.tensor.matmul(o[:, DSEQ * n:DSEQ * n + DSEQ], S0[:, n], qd[:, SEQ + DSEQ * n:SEQ + DSEQ * (n + 1)],
                                         start=(n == 0), stop=False)
                    nc.tensor.matmul(o, Vs[:], As[:], start=False, stop=True).then_inc(o_ps, 1)

                def state(c):
                    pe.wait_ge(vb_ok, hd + 1)
                    wait(pe, s1_ok, 2 * hd + c) if c else None
                    nc.tensor.matmul(aux[:, 2, :], kTs[:], Vb[:, 4 * c:4 * c + 4, :], start=True, stop=True).then_inc(s1_ps, 1)

                def onorm():
                    pe.wait_ge(s_step, 4 * hd + 4)
                    pe.wait_ge(osq_ok, 2 * hd + 2)
                    nc.tensor.matmul(aux[:, 3, :], mean_head[:], osq[:, 0:SEQ], start=True, stop=True)
                    nc.tensor.matmul(aux[:, 1, 64:64 + NS], mean_head[:], osq[:, SEQ:T], start=True, stop=True).then_inc(on_ps, 1)

                def quarter(k, mid, after):
                    if front:
                        gemm(Pos(k, t, 4), 4 * t + k, k % 2, range(DT), xh, xl, mid=mid if rec else None)
                    elif rec and mid:
                        mid()
                    if rec and after:
                        after()
                quarter(0, q0, q0b)
                quarter(1, None, lambda: gram(hd, rp, 2))
                quarter(2, lambda: (ds(), gram(hd, rp, 3)), lambda: (gram(hd, rp, 4), gram(hd, rp, 5)))
                quarter(3, lambda: gram(hd, rp, 6), lambda: (gram(hd, rp, 7), outs(), state(0), onorm(), state(1)))

            pe.wait_ge(ld_const, 80)
            gemm(Pos(0), 0, 0, range(DT), xh, xl, wait_x=(x_lo, 0))
            norm(0, DT)
            for k in range(1, 4):
                gemm(Pos(k), k, k % 2, range(DT), xh, xl)
            mixer(1, 1, True, True)
            with pe.Fori(1, 4) as i:
                mixer(2 * i, 0, True, True)
                mixer(2 * i + 1, 1, True, True)
            mixer(8, 0, False, True)

            def ffn(layer, b_in, b_out, t_in, t_out, x_base, n_norm, n_ssq, rh, rl, wait_first):
                for m in range(DT):
                    gemm(Pos(b_in - 8 + m), t_in - 8 + m, (t_in + m) % 2, range(DT), rh, rl,
                         wait_x=wait_first if m == 0 else None)
                gemm(Pos(b_in), t_in, t_in % 2, range(DT), xh, xl, wait_x=(x_lo, x_base))
                norm(n_norm, n_ssq)
                gemm(Pos(b_in + 1), t_in + 1, (t_in + 1) % 2, range(DT), xh, xl)
                for k in (2, 3):
                    gemm(Pos(b_in + k), t_in + k, (t_in + k) % 2, range(DT), xh, xl)
                with pe.Fori(1, FT // 2) as i:
                    for k in range(4):
                        gemm(Pos(b_in + k, i, 4), t_in + 4 * i + k, (t_in + k) % 2, range(DT), xh, xl)
                with pe.Fori(0, 2) as i:
                    for m in range(4):
                        for c, kts in enumerate(FO_K):
                            if m == 0:
                                pe.wait_ge(glo_ok, FT * layer + kts[-1] + 1)
                            gemm(Pos(b_out + 3 * m + c, i, 12), t_out + 4 * i + m, (t_out + m) % 2, kts, gh, glo,
                                 first=(c == 0), last=(c == 2))
            ffn(0, B_FI0, B_FO0, T_FI0, T_FO0, 8, 1, 16, oh, ol, (ol_ok, 0))
            gemm(Pos(B_KV), T_KV, T_KV % 2, range(DT), xh, xl, wait_x=(x_lo, 16))
            norm(2, 24)

            def key_mean(n):
                pe.wait_ge(ksq_ok, n + 1)
                for hf in range(2):
                    mm = nc.tensor.matmul(aux[:, hf, 0:HALF], pair_mean[:], sq[:, HALF * hf:HALF * hf + HALF], start=True, stop=True)
                mm.then_inc(km_ps, 1)

            def turn_v(k, n):
                pe.wait_ge(v2_ok, n + 1)
                wait(pe, vt_ok, 2 * n)
                turn(vT2[:, k]).then_inc(v2_ps, 1)

            def kv_pair(k, p, i, step):
                gemm(Pos(B_KV + 1 + 2 * k, i, step), T_KV + 1 + 2 * p, (T_KV + 1) % 2, range(DT), xh, xl)
                if isinstance(p, int) and p == 0:
                    pe.wait_ge(ld_kv, 64)
                    pe.wait_ge(rms_done, 3)
                    pe.wait_ge(c16_ok, 1)
                    nc.tensor.matmul(aux[:, 2, 0:NS], rep16[:], c16[:, SEQ:T], start=True, stop=True).then_inc(rep_ps, 1)
                else:
                    if isinstance(p, int) and p == 1:
                        pe.wait_ge(c_ok, 1)
                    turn_v(1 - k, p - 1)
                gemm(Pos(B_KV + 2 + 2 * k, i, step), T_KV + 2 + 2 * p, T_KV % 2, range(DT), xh, xl)
                key_mean(p)
            kv_pair(0, 0, 0, 4)
            kv_pair(1, 1, 0, 4)
            with pe.Fori(1, 4) as i:
                kv_pair(0, 2 * i, i, 4)
                kv_pair(1, 2 * i + 1, i, 4)

            def qg_pair(k, p, i, step):
                first = isinstance(p, int) and p == 0
                gemm(Pos(B_QG + 2 * k, i, step), T_QG + 2 * p, T_QG % 2, range(DT), x2h, x2l, wait_x=(x_lo, 24) if first else None)
                if first:
                    turn_v(1, 7)
                gemm(Pos(B_QG + 1 + 2 * k, i, step), T_QG + 1 + 2 * p, (T_QG + 1) % 2, range(DT), x2h, x2l)
                key_mean(p + 8)
            qg_pair(0, 0, 0, 4)
            qg_pair(1, 1, 0, 4)
            with pe.Fori(1, 4) as i:
                qg_pair(0, 2 * i, i, 4)
                qg_pair(1, 2 * i + 1, i, 4)

            idb, trib = bfc[:, 0:P], bfc[:, P:2 * P]

            def att(i):
                def score(x):
                    n, a, tb = 8 * i + x, x // 4, x % 4
                    w = P * (tb + 1)
                    if not (isinstance(i, int) and x < 2):
                        pe.wait_ge(ex_ok, n - 1)
                    s = S_ps(x % 2)
                    nc.tensor.matmul(s[:, 0:w], QX[:, a, P * tb:P * tb + P], KX[:, a, 0:w], start=True, stop=False)
                    nc.tensor.matmul(s[:, w - P:w], idb, trib, start=False, stop=True).then_inc(sc_ps, 1)

                def turn_p(x):
                    n, tb = 8 * i + x, x % 4
                    pe.wait_ge(pn_ok, n + 1)
                    if not (isinstance(i, int) and x == 0):
                        pe.wait_ge(pt_ok, n)
                    for j in range(tb + 1):
                        mm = nc.tensor.transpose(T_ps[:, P * j:P * j + P], Pr[:, x % 2, P * j:P * j + P], ident[:])
                    mm.then_inc(t_ps, 1)

                def pv(a):
                    pe.wait_ge(pt_ok, 8 * i + 4 * a + 4)
                    if a == 0:
                        wait(pe, go_ok, i)
                    for j in range(NCH):
                        mm = nc.tensor.matmul(O_ps[:, P * j:SEQ], VX[:, j, a, :], PT[:, j, P * j:SEQ],
                                              start=(a == 0 and j == 0), stop=(a == 1 and j == NCH - 1))
                    mm.then_inc(pv_ps, 1)

                pe.wait_ge(kx_ok, 8 * i + 8)
                pe.wait_ge(cx_in, 32 * i + 32)
                score(0)
                score(1)
                pe.wait_ge(kd_in, 64 * i + 64)
                pe.wait_ge(cc_ok, i + 1)
                wait(pe, dpt_ok, 2 * i)
                for hf in range(2):
                    for p in range(DT):
                        nc.tensor.matmul(D_ps[:, hf, 0:HALF], Qb[:, P * p:P * p + P], Kd[:, p, HALF * hf:HALF * hf + HALF],
                                         start=(p == 0), stop=False)
                    mm = nc.tensor.matmul(D_ps[:, hf, 0:HALF], neg_rep[:], cc[:, HALF * hf:HALF * hf + HALF], start=False, stop=(hf == 0))
                nc.tensor.matmul(D_ps[:, 1, HALF - NS:HALF], idb,
                                 bfc[:, bass.ds(2 * P + NS * i, NS)], start=False, stop=True).then_inc(d_ps, 1)
                turn_p(0)
                score(2)
                turn_p(1)
                score(3)
                turn_p(2)
                score(4)
                turn_p(3)
                pv(0)
                score(5)
                pe.wait_ge(dpn_ok, i + 1)
                for j in range(PAGES):
                    nc.tensor.transpose(D_ps[:, 0, P * j:P * j + P], Pd[:, P * j:P * j + P], ident[:])
                nc.tensor.transpose(D_ps[0:NS, 1, 0:P], Pd[:, SEQ:T], ident[:]).then_inc(dt_ps, 1)
                turn_p(4)
                score(6)
                turn_p(5)
                score(7)
                turn_p(6)
                pe.wait_ge(dpt_ok, 2 * i + 2)
                pe.wait_ge(vd_in, 64 * i + 64)
                wait(pe, dgo_ok, i)
                for p in range(DT):
                    o = O2_ps[:, p // 4, P * (p % 4):P * (p % 4) + P]
                    for j in range(PAGES):
                        nc.tensor.matmul(o, Vd[:, j, P * p:P * p + P], PTd[:, j, :], start=(j == 0), stop=False)
                    mm = nc.tensor.matmul(o, Vst[:, P * p:P * p + P], PTd[:, PAGES, :], start=False, stop=True)
                mm.then_inc(dpv_ps, 1)
                turn_p(7)
                pv(1)
            pe.wait_ge(zero_ok, 9)
            pe.wait_ge(ld_mask, 48)
            pe.wait_ge(kn_in, 1)
            pe.wait_ge(vt_ok, 16)
            pe.wait_ge(gt_ok, 8)
            att(0)
            with pe.Fori(1, 8) as i:
                att(i)
            ffn(1, B_FI1, B_FO1, T_FI1, T_FO1, 32, 3, 32, ah, al, (al_ok, 0))


def consts():
    import numpy as np
    c = np.zeros((P, N_CONST), np.float32)
    i = np.arange(P)
    c[:, C_ID:C_ID + P] = np.eye(P)
    c[:, C_MEAN:C_MEAN + P] = 1.0 / 1024
    c[:, C_HEAD:C_HEAD + P] = 1.0 / P
    c[:, C_PAIR:C_PAIR + P] = (i[:, None] // 64 == i[None, :] // 64) / 64.0
    c[:, C_NEG:C_NEG + P] = -1.0 * (i[:, None] % 16 == i[None, :] // 8)
    c[0:16, C_REP:C_REP + P] = (i[:16, None] == i[None, :] % 16)
    c[:, C_SEQ:C_SEQ + 8] = (i[:, None] // 16 == i[None, :8])
    c[0:NS, C_BLK:C_BLK + 8] = (i[:NS, None] // 8 == i[None, :8])
    t = np.arange(T)
    c[:, C_KEEP:C_KEEP + T] = np.where(t < SEQ, t % CH != 0, t % DSEQ != 0)
    c[:, C_KEEPC:C_KEEPC + T] = np.where(t < SEQ, t != 0, t % DSEQ != 0)
    m = np.zeros((P, 8, P), np.float32)
    m[:, 0] = np.eye(P)
    for j, w in enumerate(LEVELS):
        s, q = i[:, None], i[None, :]
        m[:, j + 1] = (s // (2 * w) == q // (2 * w)) & (s % (2 * w) < w) & (q % (2 * w) >= w)
    return c, m


def kernel(**inputs):
    import numpy as np
    import concourse.bacc as bacc
    from concourse.bass_utils import run_bass_kernel_spmd

    v = {k: np.asarray(a) for k, a in inputs.items()}

    def blocks(w):
        k, n = w.shape
        return w.reshape(k // P, P, n // P, P).transpose(2, 1, 0, 3).reshape(n // P, P, k)

    def vec(a):
        return a.reshape(-1, P).T

    n_phys = v["cache_k"].shape[0]
    x = np.concatenate([v["x_prompt"].reshape(SEQ, -1), v["x_sample"].reshape(NS, -1)]).T.reshape(DT, P, T)
    w_mix = blocks(v["hgrn_w_in"][0])
    order = [[8 + t, t, 16 + t, 24 + t] for t in range(HEADS)]
    w_mix = w_mix[np.array(order).reshape(-1)]
    gains = np.zeros((P, N_GAIN), np.float32)
    gains[:, G_MIX:G_MIX + 16] = vec(v["norm_mix"])
    gains[:, G_FFN:G_FFN + 16] = vec(v["norm_ffn"])
    gains[:, G_KV:G_KV + 8] = vec(v["kv_norm"])
    gains[:, G_ON] = v["hgrn_onorm"][0]
    gains[:, G_K] = np.tile(v["k_norm"], 2)
    gains[:, G_Q] = np.tile(v["q_norm"][0], 2)
    gains[0:FOX, G_BF] = v["fox_b_f"]
    gains[:, G_CW:G_CB] = vec(v["ffn_conv_w"])
    gains[:, G_CB:] = vec(v["ffn_conv_b"])
    cc, masks = consts()
    wkv = v["w_kvf"]
    wl = np.zeros((wkv.shape[0], P), np.float32)
    wl[:, 0:FOX] = wkv[:, 2048:]
    wk, wv = blocks(wkv[:, 0:1024]), blocks(wkv[:, 1024:2048])
    qg = blocks(v["fox_w_qg"][0])
    arrays = {
        "x": x, "gains": gains, "consts": cc, "masks": masks.reshape(P, 8 * P),
        "w_mix": w_mix, "w_o0": blocks(v["hgrn_w_o"][0]), "w_o1": blocks(v["fox_w_o"][0]),
        "w_kv": np.concatenate([blocks(wl)] + [w[p:p + 1] for p in range(8) for w in (wk, wv)]),
        "w_qg": np.concatenate([qg[8 * j + p:8 * j + p + 1] for p in range(8) for j in (0, 1)]),
        "s0": v["state_hgrn"][0].transpose(1, 2, 0, 3).reshape(HEADS, P, NSEQ * P),
        "conv_in": v["state_conv"].reshape(2, NSEQ, 2, FT, P).transpose(0, 4, 3, 1, 2).reshape(2, P, FT * 16),
        "pages": v["page_table"].reshape(1, -1),
        "cache_k": v["cache_k"].reshape(n_phys, P, 8, P).transpose(0, 3, 2, 1).reshape(n_phys, P, 8 * P),
        "cache_v": v["cache_v"].reshape(n_phys, P, 8 * P),
        "cache_f": v["cache_logf"].transpose(0, 2, 1),
    }
    for layer in range(2):
        w = blocks(v["ffn_w_in"][layer])
        arrays[f"w_fi{layer}"] = np.stack([w[:FT], w[FT:]], 1).reshape(2 * FT, P, 1024)
        arrays[f"w_fo{layer}"] = blocks(v["ffn_w_out"][layer])
    i = np.arange(P)
    neg = np.zeros((P, 2 * P + NSEQ * NS), np.float32)
    neg[:, 0:P] = np.eye(P)
    neg[:, P:2 * P] = np.where(i[None, :] > i[:, None], -1e30, 0.0)
    s_, n_ = np.arange(NS), np.arange(NSEQ)
    own = (s_[None, None, :] // 8 == n_[None, :, None]) & (s_[None, None, :] % 8 <= i[:, None, None] % 8)
    neg[:, 2 * P:] = np.where(own, 0.0, -1e30).reshape(P, NSEQ * NS)
    arrays["att_masks"] = neg
    arrays = {f"{k}_in": np.ascontiguousarray(a) for k, a in arrays.items()}
    outs = {"y": (DT, P, T), "k_out": (DT, P, T), "v_out": (DT, P, T), "f_out": (FOX, T), "hgrn_p": (HEADS, P, P),
            "hgrn_s": (HEADS, P, NSEQ * P), "conv_out": (2, P, FT * 18)}

    nc = bacc.Bacc("TRN2", target_bir_lowering=False, num_devices=1)
    d = {k[:-3]: nc.dram_tensor(k, a.shape, mybir.dt.from_np(a.dtype), kind="ExternalInput").ap() for k, a in arrays.items()}
    d |= {k: nc.dram_tensor(f"{k}_out", s, F32, kind="ExternalOutput").ap() for k, s in outs.items()}
    d["c_row"] = nc.dram_tensor("c_row", (FOX, T), F32, kind="Internal").ap()
    build(nc, d)
    r = run_bass_kernel_spmd(nc, [arrays], core_ids=[0]).results[0]
    r = {k: r[f"{k}_out"] for k in outs}

    def tokens(a):
        a = a.reshape(-1, T).T
        return a[:SEQ], a[SEQ:]

    yp, ys = tokens(r["y"])
    kp, ks = tokens(r["k_out"])
    vp, vs = tokens(r["v_out"])
    fp, fs = tokens(r["f_out"])
    co = r["conv_out"].reshape(2, P, FT, 18)
    return (yp.reshape(1, SEQ, 1024), ys.reshape(NSEQ, DSEQ, 1024),
            kp.reshape(1, SEQ, FOX, 64), vp.reshape(1, SEQ, FOX, 64), fp.reshape(1, SEQ, FOX),
            ks.reshape(NSEQ, DSEQ, FOX, 64), vs.reshape(NSEQ, DSEQ, FOX, 64), fs.reshape(NSEQ, DSEQ, FOX),
            r["hgrn_p"].reshape(1, 1, HEADS, P, P),
            r["hgrn_s"].reshape(HEADS, P, NSEQ, P).transpose(2, 0, 1, 3)[None],
            co[..., 0:2].transpose(0, 3, 2, 1).reshape(2, 1, 2, FT * P),
            co[..., 2:].reshape(2, P, FT, NSEQ, 2).transpose(0, 3, 4, 2, 1).reshape(2, NSEQ, 2, FT * P))
```

```python
from contextlib import ExitStack

import concourse.bass as bass
from concourse import mybir

F32 = mybir.dt.float32
F32R = mybir.dt.float32r
BF16 = mybir.dt.bfloat16
U8 = mybir.dt.uint8
I32 = mybir.dt.int32
ALU = mybir.AluOpType
ACT = mybir.ActivationFunctionType
AX = mybir.AxisListType

P = 128
SEQ = 512
NSEQ = 8
DSEQ = 8
NS = NSEQ * DSEQ
T = SEQ + NS
HALF = T // 2
DT = 8
FT = 22
HEADS = 8
FOX = 16
CH = 128
NCH = SEQ // CH
PAGES = 4
EPS = 1e-6
LEVELS = [64, 32, 16, 8, 4, 2, 1]
SAMPLE_GRAM = {3: 0, 5: 5, 6: 6, 7: 7}
RAW = 4
SPL = 2
FO_K = [list(range(0, 8)), list(range(8, 16)), list(range(16, FT))]

B_MIX, B_WO0, B_FI0, B_FO0, B_KV, B_QG, B_WO1, B_FI1, B_FO1 = 0, 32, 40, 84, 108, 125, 141, 149, 193
T_MIX, T_WO0, T_FI0, T_FO0, T_KV, T_QG, T_WO1, T_FI1, T_FO1 = 0, 32, 40, 84, 92, 109, 125, 133, 177
N_BLOCKS = 217

C_ID, C_MEAN, C_HEAD, C_PAIR, C_NEG, C_REP, C_SEQ, C_BLK, C_KEEP, C_KEEPC = 0, 128, 256, 384, 512, 640, 768, 776, 784, 1360
N_CONST = 1936
G_MIX, G_FFN, G_KV, G_ON, G_K, G_Q, G_BF, G_CW, G_CB = 0, 16, 32, 40, 41, 42, 43, 44, 44 + 2 * 3 * FT
N_GAIN = G_CB + 2 * FT


def tile_of(ap, i):
    if isinstance(i, int):
        return ap[:, i]
    return ap[:, bass.ds(i, 1)].rearrange("p a n -> p (a n)")


def row_of(ap, i):
    if isinstance(i, int):
        return ap[i]
    return ap[bass.ds(i, 1)].rearrange("a p n -> (a p) n")


def col_of(ap, i):
    return ap[:, bass.ds(i, 1)]


def wait(eng, sem, value):
    if isinstance(value, int) and value <= 0:
        return
    eng.wait_ge(sem, value)


def build(nc, d):
    ctx = ExitStack()
    with ctx:
        def sb(name, shape, dt=F32):
            return ctx.enter_context(nc.sbuf_tensor(name, shape, dt))

        def sem(name):
            return ctx.enter_context(nc.semaphore(name))

        h = sb("h", [P, DT, T])
        x_at = (nc.sbuf_base + 31) // 32 * 32
        xh = sb("xh", [P, DT, T], F32R)
        xl = sb("xl", [P, DT, T], F32R)
        w_raw = sb("w_raw", [P, RAW, 1024])
        w_hi = sb("w_hi", [P, SPL, 1024], F32R)
        w_lo = sb("w_lo", [P, SPL, 1024], F32R)
        ident = sb("ident", [P, P])
        mean_all = sb("mean_all", [P, P])
        gains = sb("gains", [P, N_GAIN])
        rms = sb("rms", [P, T])
        sq = sb("sq", [P, T])
        ssq = sb("ssq", [P, T])
        eps = sb("eps", [P, 1])
        base = (nc.sbuf_base + 63) // 64 * 64
        end = nc.sbuf_usable_end

        class Region:
            def __init__(self, tag, offset=base):
                self.tag, self.at = tag, offset

            def __call__(self, name, shape, dt=F32, size=4):
                n = size
                for s in shape[1:]:
                    n *= s
                t = nc.alloc_sbuf_tensor_at(f"{self.tag}_{name}", shape, dt, offset=self.at)
                self.at += (n + 63) // 64 * 64
                assert self.at <= end, (self.tag, name, self.at, end)
                return t

        mx = Region("mix")
        oh = mx("oh", [P, DT, T], F32R)
        ol = mx("ol", [P, DT, T], F32R)
        keep = mx("keep", [P, T])
        mean_head = mx("mean_head", [P, P])
        masks = mx("masks", [P, 8, P], U8, 1)
        blk = mx("blk", [P, 8])
        fr = mx("fr", [P, T]); fl = mx("fl", [P, T])
        qr = mx("qr", [P, T]); ql = mx("ql", [P, T])
        gr = mx("gr", [P, T]); gl = mx("gl", [P, T]); gate = mx("gate", [P, T])
        kd0 = fr
        b_ = mx("b", [P, 2, T]); k_ = mx("k", [P, 2, T]); q_ = mx("q", [P, 2, T])
        vT = mx("vT", [P, T])
        eb = mx("eb", [P, T]); qd = mx("qd", [P, T]); kd = mx("kd", [P, T])
        E = mx("E", [P, 2, T]); Z = mx("Z", [P, 2, T])
        A = mx("A", [P, NCH, P]); As = mx("As", [NS, NS])
        V = mx("V", [P, NCH, P]); Vs = mx("Vs", [NS, P]); Vb = mx("Vb", [P, NSEQ, P])
        kT = mx("kT", [P, NCH, P]); kTs = mx("kTs", [P, P])
        S = mx("S", [P, NCH, P])
        S0 = mx("S0", [P, NSEQ, P]); S1 = mx("S1", [P, NSEQ, P])
        orr = mx("orr", [P, T]); og = mx("og", [P, T])
        osq = og

        ff = Region("ffn")
        gh = ff("gh", [P, FT, T], F32R)
        glo = ff("glo", [P, FT, T], F32R)
        UW = 2 + SEQ + NSEQ * (2 + DSEQ)
        u = ff("u", [P, UW])
        a_ = ff("a", [P, T]); sil = ff("sil", [P, T])
        cst = ff("cst", [P, FT * 18])
        cin = ff("cin", [P, FT * 16])

        kv = Region("kv")
        x2h = kv("x2h", [P, DT, T], F32R)
        x2l = kv("x2l", [P, DT, T], F32R)
        KT = kv("KT", [P, DT, T])
        Vt = kv("Vt", [P, NCH, 8 * P])
        Vst = kv("Vst", [P, 8 * P])
        q_at = kv.at
        QT = kv("QT", [P, DT, T])
        GT = kv("GT", [P, DT, T])
        pair_mean = kv("pair_mean", [P, P])
        seq_col = kv("seq_col", [P, 8])
        gq = kv("gq", [P, 1])
        pg = kv("pg", [1, NSEQ * PAGES], I32)
        gate_log = kv("gate_log", [P, T])
        C = ssq
        t1 = Region("kvt", q_at)
        CL = t1("CL", [P, SEQ]); keep_c = t1("keep_c", [P, T])
        fx = t1("fx", [FOX, T]); fe = t1("fe", [FOX, T]); c16 = t1("c16", [FOX, T])
        c16h = t1("c16h", [FOX, T], F32R); c16l = t1("c16l", [FOX, T], F32R)
        rep16 = t1("rep16", [FOX, P])
        assert t1.at <= q_at + DT * T * 4
        t2 = Region("kvu", q_at + DT * T * 4)
        vT2 = t2("vT2", [P, 2, T])
        t3 = Region("dec", x_at)
        Kd = t3("Kd", [P, DT, T])
        Vd = t3("Vd", [P, PAGES, 8 * P])
        neg_rep = t3("neg_rep", [P, P])
        bfc = t3("bfc", [P, 2 * P + NSEQ * NS], BF16, 2)
        assert t3.at <= x_at + 2 * DT * T * 4
        t4 = Region("att")
        QX = t4("QX", [P, 2, 2, SEQ])
        cX = t4("cX", [4, 2, SEQ], F32R)
        sel = t4("sel", [4, 2, P], F32R)
        Pr = t4("Pr", [P, 2, SEQ]); wide_at = t4.at; PT = t4("PT", [P, 2, NCH, P]); OT = t4("OT", [P, NCH, P])
        Qb = t4("Qb", [P, 8 * 144]); Pd = t4("Pd", [P, T]); PTd = t4("PTd", [P, PAGES + 1, P])
        cc = t4("cc", [P, T])
        nm = t4("nm", [P, 8]); rs = t4("rs", [P, 8]); rr = t4("rr", [P, 8]); dm = t4("dm", [P, 4])
        assert t4.at <= base + 2 * DT * T * 4, t4.at - base
        t6 = Region("wide", wide_at)
        wide = t6("masks", [P, 4 * P + NSEQ * NS])
        t5 = Region("ao")
        ah = t5("ah", [P, DT, T], F32R); al = t5("al", [P, DT, T], F32R)

        acc = ctx.enter_context(nc.psum_tensor("acc", [P, 2, 2, 512], F32))
        aux = ctx.enter_context(nc.psum_tensor("aux", [P, 4, 512], F32))

        def S_ps(k):
            return acc[:, 0, k]
        T_ps, O_ps, D_ps, O2_ps, U_ps = acc[:, 1, 0], acc[:, 1, 1], aux[:, 0:2], aux[:, 2], aux[:, 3]

        w_in = [sem(f"w_in{i}") for i in range(RAW)]
        hi_done, lo_done, block_done, evac = sem("hi_done"), sem("lo_done"), sem("block_done"), sem("evac")
        ld_const, ld_gain, ld_mask = sem("ld_const"), sem("ld_gain"), sem("ld_mask")
        ld_h = [sem(f"ld_h{i}") for i in range(DT)]
        x_hi, x_lo, sq_done, ssq_done = sem("x_hi"), sem("x_lo"), sem("sq_done"), sem("ssq_done")
        norm_ps, ln_done, rms_done = sem("norm_ps"), sem("ln_done"), sem("rms_done")
        setup = sem("setup")
        fr_ok, f_t, lf_ok, b_ok, kd0_ok, k_ok = [sem(n) for n in ("fr_ok", "f_t", "lf_ok", "b_ok", "kd0_ok", "k_ok")]
        qr_ok, q_t, ql_ok, q_sig, q_ok = [sem(n) for n in ("qr_ok", "q_t", "ql_ok", "q_sig", "q_ok")]
        gr_ok, g_t, gl_ok, g_sig, gate_ok = [sem(n) for n in ("gr_ok", "g_t", "gl_ok", "g_sig", "gate_ok")]
        vT_ok = sem("vT_ok")
        kdd_ok, kde_ok, eb_ok, kd_ok, qd_ok = [sem(n) for n in ("kdd_ok", "kde_ok", "eb_ok", "kd_ok", "qd_ok")]
        vT_ps, v_ok, vb_ok, kT_ps, kT_ok = [sem(n) for n in ("vT_ps", "v_ok", "vb_ok", "kT_ps", "kT_ok")]
        diff_ok, exp_ok, z_ok, gram_ps, gram_used = [sem(n) for n in ("diff_ok", "exp_ok", "z_ok", "gram_ps", "gram_used")]
        ds_ps, s_step, s_ok, o_ps, osq_ok, on_ps, oln_ok, orr_ok, og_ok, ogg_ok, oh_ok, ol_ok = [sem(n) for n in (
            "ds_ps", "s_step", "s_ok", "o_ps", "osq_ok", "on_ps", "oln_ok", "orr_ok", "og_ok", "ogg_ok", "oh_ok", "ol_ok")]
        s0_in, s0_mul, s1_ps, s1_ok, s1_out, s_out = [sem(n) for n in ("s0_in", "s0_mul", "s1_ps", "s1_ok", "s1_out", "s_out")]
        st_in, ubuf_ok, u_ok, c0_ok, c2_ok, sil_ok, silr_ok, prod_ok, gh_ok, glo_ok, cst_ok = [sem(n) for n in (
            "st_in", "ubuf_ok", "u_ok", "c0_ok", "c2_ok", "sil_ok", "silr_ok", "prod_ok", "gh_ok", "glo_ok", "cst_ok")]
        out_cst = sem("out_cst")
        h_ok, taking = sem("h_ok"), sem("taking")
        ld_kv, pg_in, cl_in, fx_ok, fb_ok, fe_t, flf_ok, c16_ok, f_out, c_scan, rep_ps, c_ok, c_dram = [sem(n) for n in (
            "ld_kv", "pg_in", "cl_in", "fx_ok", "fb_ok", "fe_t", "flf_ok", "c16_ok", "f_out", "c_scan", "rep_ps", "c_ok", "c_dram")]
        gq_ok, kr_ok, ksq_ok, km_ps, kln_ok, krk_ok, kn_ok, v2_ok, v2_ps, vt_ok, z_set = [sem(n) for n in (
            "gq_ok", "kr_ok", "ksq_ok", "km_ps", "kln_ok", "krk_ok", "kn_ok", "v2_ok", "v2_ps", "vt_ok", "z_set")]
        k_out, v_out = [sem("k_out0"), sem("k_out1")], [sem("v_out0"), sem("v_out1")]
        gx_ok, gx_t, gx_ls, gt_ok = [sem(n) for n in ("gx_ok", "gx_t", "gx_ls", "gt_ok")]
        cx_in = [sem("cx_in0"), sem("cx_in1")]
        qx_ok, sc_ps, mx_ok, ex_ok, rc_ok, t_ps, pt_ok, pv_ps, ov_ok, u_ps, go_ok, ch_ok, cl_ok = [sem(n) for n in (
            "qx_ok", "sc_ps", "mx_ok", "ex_ok", "rc_ok", "t_ps", "pt_ok", "pv_ps", "ov_ok", "u_ps", "go_ok", "ch_ok", "cl_ok")]
        kd_in, vd_in, kn_in, qb_ok, cc_ok, d_ps, dmx_ok, dex_ok, drc_ok, dpn_ok, dt_ps, dpt_ok, dpv_ps, dgo_ok, zero_ok = [
            sem(n) for n in ("kd_in", "vd_in", "kn_in", "qb_ok", "cc_ok", "d_ps", "dmx_ok", "dex_ok", "drc_ok", "dpn_ok",
                             "dt_ps", "dpt_ok", "dpv_ps", "dgo_ok", "zero_ok")]
        ah_ok, al_ok, y_out = sem("ah_ok"), sem("al_ok"), sem("y_out")

        def halves(ap):
            return ap.rearrange("p (a n) -> p a n", a=2)

        def level(ap, m):
            w = T if m <= 4 else SEQ
            return ap[:, 0:w].rearrange("p (n two m) -> p n two m", two=2, m=m)

        block = ctx.enter_context(nc.Block())

        class Pos:
            def __init__(self, b0, i=0, step=0):
                assert step % RAW == 0
                self.b, self.slot, self.lap = b0 + step * i, b0 % RAW, b0 // RAW + (step // RAW) * i

        @block.sync
        def _(sp):
            sp.dma_start(h[:, 0, :], d["x"][0]).then_inc(ld_h[0], 16)
            sp.dma_start(gains[:], d["gains"]).then_inc(ld_gain, 16)

            def load(pos, src, width=1024):
                wait(sp, lo_done, pos.b - RAW + 1)
                sp.dma_start(w_raw[:, pos.slot, 0:width], src).then_inc(w_in[pos.slot], 16)

            def mixer(t, i0, i):
                for j in range(4):
                    load(Pos(B_MIX + 4 * i0 + j, i, 4), row_of(d["w_mix"], 4 * t + j))

            load(Pos(0), d["w_mix"][0])
            for m in range(1, DT):
                sp.dma_start(h[:, m, :], d["x"][m]).then_inc(ld_h[m], 16)
                if m == 4:
                    load(Pos(1), d["w_mix"][1])
            sp.dma_start(ident[:], d["consts"][:, C_ID:C_ID + P]).then_inc(ld_const, 16)
            sp.dma_start(mean_all[:], d["consts"][:, C_MEAN:C_MEAN + P]).then_inc(ld_const, 16)
            sp.dma_start(mean_head[:], d["consts"][:, C_HEAD:C_HEAD + P]).then_inc(ld_const, 16)
            sp.dma_start(blk[:], d["consts"][:, C_BLK:C_BLK + 8]).then_inc(ld_const, 16)
            sp.dma_start(keep[:], d["consts"][:, C_KEEP:C_KEEP + T]).then_inc(ld_const, 16)
            sp.dma_start(Z[:].rearrange("p a n -> p (a n)")[:, 0:8 * P], d["masks"]).then_inc(ld_mask, 16)
            for j in range(2, 4):
                load(Pos(j), d["w_mix"][j])
            with sp.Fori(1, HEADS) as t:
                mixer(t, 0, t)

            def plain(b0, n, w):
                with sp.Fori(0, n // 4) as i:
                    for j in range(4):
                        load(Pos(b0 + j, i, 4), row_of(w, 4 * i + j))

            def ffn(layer, b_in, b_out):
                plain(b_in, 2 * FT, d[f"w_fi{layer}"])
                with sp.Fori(0, 2) as i:
                    for m in range(4):
                        for c, kts in enumerate(FO_K):
                            w = 128 * len(kts)
                            load(Pos(b_out + 3 * m + c, i, 12), row_of(d[f"w_fo{layer}"], 4 * i + m)[:, 1024 * c:1024 * c + w], w)

            plain(B_WO0, 8, d["w_o0"])
            ffn(0, B_FI0, B_FO0)
            for j in range(4):
                load(Pos(B_KV + j), d["w_kv"][j])
            sp.wait_ge(block_done, B_KV)
            sp.wait_ge(out_cst, 16)
            sp.dma_start(pg[:], d["pages"]).then_inc(pg_in, 16)
            for dst, src in ((pair_mean[:], d["consts"][:, C_PAIR:C_PAIR + P]),
                             (seq_col[:], d["consts"][:, C_SEQ:C_SEQ + 8]), (keep_c[:], d["consts"][:, C_KEEPC:C_KEEPC + T]),
                             (rep16[:], d["consts"][0:FOX, C_REP:C_REP + P])):
                sp.dma_start(dst, src).then_inc(ld_kv, 16)
            sp.wait_ge(pg_in, 16)
            n_phys = d["cache_f"].shape[0]

            def page(n, j):
                return sp.value_load(pg[0:1, bass.ds(PAGES * n + j, 1)], min_val=0, max_val=n_phys - 1)

            for i in range(1, 4):
                for j in range(4):
                    load(Pos(B_KV + j, i, 4), d["w_kv"][4 * i + j])
                for n in range(3 * (i - 1), min(3 * i, NSEQ)):
                    for j in range(PAGES):
                        sp.dma_start(CL[FOX * n:FOX * n + FOX, P * j:P * j + P], row_of(d["cache_f"], page(n, j)))\
                            .then_inc(cl_in, 16)
            load(Pos(B_KV + 16), d["w_kv"][16])

            def pages(n):
                at = [page(n, j) for j in range(PAGES)]
                wait(sp, d_ps, n)
                for j in range(PAGES):
                    sp.dma_start(Kd[:, :, P * j:P * j + P],
                                 row_of(d["cache_k"], at[j]).rearrange("p (a s) -> p a s", a=8)).then_inc(kd_in, 16)
                wait(sp, dpv_ps, 2 * n)
                for j in range(PAGES):
                    sp.dma_start(Vd[:, j, :], row_of(d["cache_v"], at[j])).then_inc(vd_in, 16)

            for j in range(4):
                load(Pos(B_QG + j), d["w_qg"][j])
            with sp.Fori(1, 3) as i:
                for j in range(4):
                    load(Pos(B_QG + j, i, 4), row_of(d["w_qg"], 4 * i + j))
            sp.wait_ge(block_done, B_QG)
            sp.dma_start(neg_rep[:], d["consts"][:, C_NEG:C_NEG + P]).then_inc(ld_mask, 16)
            pages(0)
            for j in range(4):
                load(Pos(B_QG + 12 + j), d["w_qg"][12 + j])
            for j in range(4):
                load(Pos(B_WO1 + j), d["w_o1"][j])
            sp.wait_ge(block_done, B_WO1)
            sp.dma_start(wide[:], d["att_masks"]).then_inc(ld_mask, 16)
            with sp.Fori(1, NSEQ) as n:
                pages(n)
            for j in range(4, 8):
                load(Pos(B_WO1 + j), d["w_o1"][j])
            ffn(1, B_FI1, B_FO1)

        @block.scalar
        def _(act):
            def hi(pos, width=1024):
                wait(act, block_done, pos.b - SPL + 1)
                act.wait_ge(w_in[pos.slot], 16 * pos.lap + 16)
                nc.scalar.activation(w_hi[:, pos.slot % SPL, 0:width], w_raw[:, pos.slot, 0:width], ACT.Copy)\
                    .then_inc(hi_done, 1)

            def square(n, m):
                if m == 0:
                    wait(act, norm_ps, n // DT)
                    nc.scalar.activation(ssq[:], h[:, 0, :], ACT.Square).then_inc(sq_done, 1)
                else:
                    wait(act, ssq_done, n)
                    nc.scalar.activation(sq[:], tile_of(h, m), ACT.Square).then_inc(sq_done, 1)

            def gain_hi(dst, m, g):
                nc.scalar.activation(tile_of(dst, m), tile_of(h, m), ACT.Copy, scale=col_of(gains, g + m)).then_inc(x_hi, 1)

            def stats(n):
                act.wait_ge(norm_ps, n + 1)
                nc.scalar.activation(halves(sq[:]), aux[:, 0:2, 0:HALF], ACT.Ln, bias=eps[:, 0:1]).then_inc(ln_done, 1)
                act.wait_ge(ln_done, n + 1)
                nc.scalar.activation(rms[:], sq[:], ACT.Exp, scale=-0.5).then_inc(rms_done, 1)

            def softlog(src, dst, ready, done, n, *used):
                for s in used:
                    wait(act, s, n)
                act.wait_ge(ready, n + 1)
                nc.scalar.activation(dst[:], src[:], ACT.Abs).then_inc(done, 1)
                act.wait_ge(done, 3 * n + 1)
                nc.scalar.activation(dst[:], dst[:], ACT.Exp, scale=-1.0).then_inc(done, 1)
                act.wait_ge(done, 3 * n + 2)
                nc.scalar.activation(dst[:], dst[:], ACT.Ln, bias=1.0).then_inc(done, 1)

            def rec_exp(hd, j):
                w = T if LEVELS[j] <= 4 else SEQ
                act.wait_ge(diff_ok, 7 * hd + j + 1)
                nc.scalar.activation(E[:, j % 2, 0:w], E[:, j % 2, 0:w], ACT.Exp).then_inc(exp_ok, 1)

            def mixer(t, par, front, rec, tail):
                hd, td = t - 1, t - 2
                if front:
                    hi(Pos(1, t, 4))
                if rec:
                    softlog(gr, gl, gr_ok, g_t, hd, gate_ok)
                    act.wait_ge(b_ok, hd + 1)
                    wait(act, s_step, 4 * hd)
                    wait(act, s0_mul, hd)
                    nc.scalar.activation(eb[:], b_[:, 1 - par, :], ACT.Exp).then_inc(eb_ok, 1)
                    act.wait_ge(kdd_ok, hd + 1)
                    nc.scalar.activation(kd[:], kd[:], ACT.Exp).then_inc(kde_ok, 1)
                    rec_exp(hd, 0)
                if tail:
                    act.wait_ge(o_ps, td + 1)
                    nc.scalar.activation(osq[:, 0:SEQ], aux[:, 0, :], ACT.Square).then_inc(osq_ok, 1)
                    nc.scalar.activation(osq[:, SEQ:T], aux[:, 1, 0:NS], ACT.Square).then_inc(osq_ok, 1)
                if rec:
                    rec_exp(hd, 1)
                    act.wait_ge(gl_ok, hd + 1)
                    nc.scalar.activation(gl[:], gl[:], ACT.Exp).then_inc(g_sig, 1)
                if tail:
                    act.wait_ge(on_ps, td + 1)
                    nc.scalar.activation(orr[:, 0:SEQ], aux[:, 3, :], ACT.Ln, bias=eps[:, 0:1]).then_inc(oln_ok, 1)
                    nc.scalar.activation(orr[:, SEQ:T], aux[:, 1, 64:64 + NS], ACT.Ln, bias=eps[:, 0:1]).then_inc(oln_ok, 1)
                    act.wait_ge(oln_ok, 2 * td + 2)
                    nc.scalar.activation(orr[:], orr[:], ACT.Exp, scale=-0.5).then_inc(orr_ok, 1)
                if front:
                    hi(Pos(2, t, 4))
                    softlog(fr, fl, fr_ok, f_t, t, b_ok, kd0_ok)
                if tail:
                    act.wait_ge(ogg_ok, td + 1)
                    nc.scalar.activation(tile_of(oh, td), og[:], ACT.Copy).then_inc(oh_ok, 1)
                if rec:
                    rec_exp(hd, 2)
                if front:
                    act.wait_ge(kd0_ok, t + 1)
                    nc.scalar.activation(k_[:, par, :], kd0[:], ACT.Exp).then_inc(k_ok, 1)
                if rec:
                    act.wait_ge(vT_ps, hd + 1)
                    nc.scalar.activation(V[:], aux[:, 3, :].rearrange("p (c s) -> p c s", c=NCH), ACT.Copy).then_inc(v_ok, 1)
                    nc.scalar.activation(Vs[:], aux[0:NS, 2, 0:P], ACT.Copy).then_inc(v_ok, 1)
                if front:
                    hi(Pos(3, t, 4))
                if rec:
                    rec_exp(hd, 3)
                    act.wait_ge(kT_ps, hd + 1)
                    nc.scalar.activation(kT[:], aux[:, 3, :].rearrange("p (c s) -> p c s", c=NCH), ACT.Copy).then_inc(kT_ok, 1)
                    nc.scalar.activation(kTs[0:NS, :], aux[0:NS, 2, 0:P], ACT.Copy).then_inc(kT_ok, 1)
                if front:
                    softlog(qr, ql, qr_ok, q_t, t, q_ok)
                if rec:
                    rec_exp(hd, 4)
                if front:
                    hi(Pos(4, t, 4))
                    act.wait_ge(ql_ok, t + 1)
                    nc.scalar.activation(ql[:], ql[:], ACT.Exp).then_inc(q_sig, 1)
                if rec:
                    rec_exp(hd, 5)
                    rec_exp(hd, 6)

            def out_tile(m, n_h, n_x, n_s, g):
                act.wait_ge(h_ok, n_h)
                square(n_s, m)
                if g is not None:
                    gain_hi(xh, m, g)

            nc.scalar.preload_act_table_set("natural_log_exp_and_others")
            act.wait_ge(setup, 1)
            act.wait_ge(ld_gain, 16)
            for m in range(DT):
                act.wait_ge(ld_h[m], 16)
                gain_hi(xh, m, G_MIX)
                if m == 0:
                    hi(Pos(0))
                wait(act, ssq_done, m - 1)
                nc.scalar.activation((ssq, sq, rms)[m and 2 - m % 2][:], h[:, m, :], ACT.Square).then_inc(sq_done, 1)
                if m == 6:
                    hi(Pos(1))
            stats(0)
            def stage0():
                hi(Pos(2))
                softlog(fr, fl, fr_ok, f_t, 0)
                hi(Pos(3))
                act.wait_ge(kd0_ok, 1)
                nc.scalar.activation(k_[:, 0, :], kd0[:], ACT.Exp).then_inc(k_ok, 1)
                softlog(qr, ql, qr_ok, q_t, 0)
                hi(Pos(4))
                act.wait_ge(ql_ok, 1)
                nc.scalar.activation(ql[:], ql[:], ACT.Exp).then_inc(q_sig, 1)
            stage0()
            mixer(1, 1, True, True, False)
            with act.Fori(1, 4) as i:
                mixer(2 * i, 0, True, True, True)
                mixer(2 * i + 1, 1, True, True, True)
            mixer(8, 0, False, True, True)
            mixer(9, 1, False, False, True)

            def ffn(layer, b_in, b_out, g_next, n_norm, h_base, s_base):
                n_h0 = h_base
                for m in range(DT):
                    if m or layer == 0:
                        hi(Pos(b_in - 8 + m + 1))
                    out_tile(m, n_h0 + m + 1, None, s_base + m, G_FFN + 8 * layer)
                hi(Pos(b_in + 1))
                stats(n_norm)
                nc.scalar.preload_act_table_set("silu_and_others")
                def pair(k, i):
                    f = 2 * i + k
                    n = FT * layer + f
                    act.wait_ge(u_ok, n + 1)
                    cw = G_CW + 3 * FT * layer
                    for dst, src in ((a_[:, 0:SEQ], u[:, 2:2 + SEQ]),
                                     (a_[:, SEQ:T].rearrange("p (n t) -> p n t", n=NSEQ),
                                      u[:, 2 + SEQ:UW].rearrange("p (n t) -> p n t", n=NSEQ)[:, :, 2:])):
                        nc.scalar.activation(dst, src, ACT.Identity, scale=col_of(gains, cw + 2 * FT + f),
                                             bias=col_of(gains, G_CB + FT * layer + f)).then_inc(c0_ok, 1)
                    hi(Pos(b_in + 2 * k + 2, i, 4))
                    act.wait_ge(c2_ok, 2 * n + 2)
                    nc.scalar.activation(sil[:], a_[:], ACT.Silu).then_inc(sil_ok, 1)
                    hi(Pos(b_in + 2 * k + 3, i, 4))
                    act.wait_ge(prod_ok, n + 1)
                    nc.scalar.activation(tile_of(gh, f), sil[:], ACT.Copy).then_inc(gh_ok, 1)
                pair(0, 0)
                pair(1, 0)
                with act.Fori(1, FT // 2) as i:
                    pair(0, i)
                    pair(1, i)
                nc.scalar.preload_act_table_set("natural_log_exp_and_others")
                def body(i, last):
                    for m4 in range(4):
                        for c in range(3):
                            if not (last and m4 == 3 and c == 2) and not (isinstance(i, int) and i == m4 == c == 0):
                                nxt = (c + 1) % 3
                                hi(Pos(b_out + 3 * m4 + c + 1, i, 12), 128 * len(FO_K[nxt]) if not (m4 == 3 and c == 2) else 1024)
                        m = 4 * i + m4
                        act.wait_ge(h_ok, n_h0 + 8 + m + 1)
                        if g_next is not None:
                            if isinstance(i, int) and m == 0:
                                nc.scalar.activation(ssq[:], h[:, 0, :], ACT.Square).then_inc(sq_done, 1)
                            else:
                                act.wait_ge(ssq_done, s_base + 8 + m)
                                nc.scalar.activation(sq[:], tile_of(h, m), ACT.Square).then_inc(sq_done, 1)
                            gain_hi(xh, m, g_next)
                body(0, False)
                body(1, g_next is None)
            ffn(0, B_FI0, B_FO0, G_KV, 1, 0, 8)
            def key_norm(src, p, n, split=None):
                act.wait_ge(kr_ok, n + 1)
                nc.scalar.activation(sq[:], tile_of(src, p), ACT.Square).then_inc(ksq_ok, 1)
                if split is not None:
                    hi(split)
                act.wait_ge(km_ps, n + 1)
                nc.scalar.activation(halves(sq[:]), aux[:, 0:2, 0:HALF], ACT.Ln, bias=eps[:, 0:1]).then_inc(kln_ok, 1)
                wait(act, kn_ok, n)
                act.wait_ge(kln_ok, n + 1)
                nc.scalar.activation(sq[:], sq[:], ACT.Exp, scale=-0.5).then_inc(krk_ok, 1)

            def value_out(p, n):
                act.wait_ge(v2_ps, n + 1)
                nc.scalar.activation(Vt[:, :, bass.ds(P * p, P)], aux[:, 3, :].rearrange("p (c s) -> p c s", c=NCH), ACT.Copy)\
                    .then_inc(vt_ok, 1)
                nc.scalar.activation(Vst[0:NS, bass.ds(P * p, P)], aux[0:NS, 2, 0:P], ACT.Copy).then_inc(vt_ok, 1)

            hi(Pos(B_KV + 1))
            stats(2)
            act.wait_ge(fb_ok, 1)
            nc.scalar.activation(fe[:], fx[:], ACT.Abs).then_inc(fe_t, 1)
            act.wait_ge(fe_t, 1)
            nc.scalar.activation(fe[:], fe[:], ACT.Exp, scale=-1.0).then_inc(fe_t, 1)
            act.wait_ge(fe_t, 2)
            nc.scalar.activation(fe[:], fe[:], ACT.Ln, bias=1.0).then_inc(fe_t, 1)

            def kv_pair(k, p, i, step, first):
                hi(Pos(B_KV + 2 + 2 * k, i, step))
                if not first:
                    value_out(p - 1, p - 1)
                gain_hi(x2h, p, G_MIX + DT)
                hi(Pos(B_KV + 3 + 2 * k, i, step))
                key_norm(KT, p, p)
            kv_pair(0, 0, 0, 4, True)
            kv_pair(1, 1, 0, 4, False)
            with act.Fori(1, 4) as i:
                kv_pair(0, 2 * i, i, 4, False)
                kv_pair(1, 2 * i + 1, i, 4, False)

            def qg_pair(k, p, i, step, last_split):
                if isinstance(p, int) and p == 0:
                    hi(Pos(B_QG + 1))
                    value_out(7, 7)
                hi(Pos(B_QG + 2 + 2 * k, i, step))
                key_norm(QT, p, p + 8, Pos(B_QG + 3 + 2 * k, i, step))
                g = tile_of(GT, p)
                act.wait_ge(gx_ok, p + 1)
                wait(act, gx_ls, p)
                nc.scalar.activation(gate_log[:], g, ACT.Abs).then_inc(gx_t, 1)
                act.wait_ge(gx_t, 3 * p + 1)
                nc.scalar.activation(gate_log[:], gate_log[:], ACT.Exp, scale=-1.0).then_inc(gx_t, 1)
                act.wait_ge(gx_t, 3 * p + 2)
                nc.scalar.activation(gate_log[:], gate_log[:], ACT.Ln, bias=1.0).then_inc(gx_t, 1)
                act.wait_ge(rms_done, 3)
                act.wait_ge(gx_ls, p + 1)
                nc.scalar.activation(g, g, ACT.Exp).then_inc(gt_ok, 1)
            qg_pair(0, 0, 0, 4, False)
            qg_pair(1, 1, 0, 4, False)
            with act.Fori(1, 4) as i:
                qg_pair(0, 2 * i, i, 4, False)
                qg_pair(1, 2 * i + 1, i, 4, False)

            def att(i, cur, prev):
                def ex(x):
                    n = 8 * i + x
                    w = P * (x % 4 + 1)
                    act.wait_ge(mx_ok, n + 1)
                    if not (isinstance(i, int) and n < 2):
                        act.wait_ge(t_ps, n - 1)
                    if not (isinstance(i, int) and n < 8):
                        act.wait_ge(rc_ok, n - 7)
                    nc.scalar.activation(Pr[:, x % 2, 0:w], S_ps(x % 2)[:, 0:w], ACT.Exp, bias=nm[:, x:x + 1],
                                         accum_out=rs[:, x:x + 1]).then_inc(ex_ok, 1)

                def tcopy(x):
                    n = 8 * i + x
                    tb = x % 4
                    act.wait_ge(t_ps, n + 1)
                    if not (isinstance(i, int) and n < 2):
                        act.wait_ge(pv_ps, n - 1)
                    nc.scalar.activation(PT[:, x % 2, 0:tb + 1, :],
                                         T_ps[:, 0:P * (tb + 1)].rearrange("p (c s) -> p c s", c=tb + 1), ACT.Copy)\
                        .then_inc(pt_ok, 1)

                if prev:
                    act.wait_ge(dmx_ok, i)
                    if not (isinstance(i, int) and i < 2):
                        act.wait_ge(dt_ps, i - 1)
                    nc.scalar.activation(halves(Pd[:]), D_ps[:, :, 0:HALF], ACT.Exp, bias=dm[:, 0:1],
                                         accum_out=dm[:, 1:2]).then_inc(dex_ok, 1)
                if cur:
                    ex(0)
                if prev:
                    tcopy(-1)
                if cur:
                    ex(1)
                if prev:
                    act.wait_ge(dt_ps, i)
                    if not (isinstance(i, int) and i < 2):
                        act.wait_ge(dpv_ps, 2 * i - 2)
                    nc.scalar.activation(PTd[:, 0:PAGES, :], D_ps[:, 0, :].rearrange("p (c s) -> p c s", c=PAGES), ACT.Copy)\
                        .then_inc(dpt_ok, 1)
                    nc.scalar.activation(PTd[0:NS, PAGES, :], D_ps[0:NS, 1, 0:P], ACT.Copy).then_inc(dpt_ok, 1)
                if cur:
                    for x in range(2, 8):
                        tcopy(x - 2)
                        ex(x)
                    tcopy(6)
            att(0, True, False)
            act.wait_ge(zero_ok, 5)
            att(1, True, True)
            with act.Fori(1, 4) as i:
                att(2 * i, True, True)
                att(2 * i + 1, True, True)
            att(8, False, True)
            act.wait_ge(go_ok, 8)
            act.wait_ge(dgo_ok, 16)
            for p in range(DT):
                nc.scalar.activation(ah[:, p, :], GT[:, p, :], ACT.Copy).then_inc(ah_ok, 1)
            ffn(1, B_FI1, B_FO1, None, 3, 16, 24)

        @block.vector
        def _(dve):
            def lo(pos, width=1024):
                dve.wait_ge(hi_done, pos.b + 1)
                nc.vector.tensor_tensor(w_lo[:, pos.slot % SPL, 0:width], w_raw[:, pos.slot, 0:width],
                                        w_hi[:, pos.slot % SPL, 0:width].bitcast(F32), ALU.subtract).then_inc(lo_done, 1)

            def gain_lo(dst, src_hi, m, g, n):
                dve.wait_ge(x_hi, n + 1)
                nc.vector.scalar_tensor_tensor(out=tile_of(dst, m), in0=tile_of(h, m), scalar=col_of(gains, g + m),
                                               in1=tile_of(src_hi, m).bitcast(F32), op0=ALU.mult, op1=ALU.subtract)\
                    .then_inc(x_lo, 1)

            def scaled(dst, b, tp, done):
                dve.wait_ge(block_done, b + 1)
                nc.vector.tensor_tensor(halves(dst), acc[:, tp, :, 0:HALF], halves(rms[:]), ALU.mult).then_inc(done, 1)

            def logsig(x, l, ready, done, n):
                dve.wait_ge(ready, 3 * n + 3)
                nc.vector.scalar_tensor_tensor(out=l[:], in0=x[:], scalar=0.0, in1=l[:], op0=ALU.min, op1=ALU.subtract)\
                    .then_inc(done, 1)

            def diff(hd, rp, j):
                m = LEVELS[j]
                bv, ev = level(b_[:, rp], m), level(E[:, j % 2], m)
                mid = bv[:, :, 0, m - 1:m]
                n = bv.shape[1]
                wait(dve, z_ok, 7 * hd + j - 1)
                nc.vector.tensor_tensor(ev[:, :, 1, :], bv[:, :, 1, :], mid.to_broadcast([P, n, m]), ALU.subtract)
                nc.vector.tensor_tensor(ev[:, :, 0, :], mid.to_broadcast([P, n, m]), bv[:, :, 0, :], ALU.subtract)\
                    .then_inc(diff_ok, 1)

            def zed(hd, rp, j):
                m = LEVELS[j]
                kv, qv = level(k_[:, rp], m), level(q_[:, rp], m)
                ev, zv = level(E[:, j % 2], m), level(Z[:, j % 2], m)
                dve.wait_ge(exp_ok, 7 * hd + j + 1)
                nc.vector.tensor_tensor(zv[:, :, 1, :], qv[:, :, 1, :], ev[:, :, 1, :], ALU.mult)
                nc.vector.tensor_tensor(zv[:, :, 0, :], kv[:, :, 0, :], ev[:, :, 0, :], ALU.mult).then_inc(z_ok, 1)

            def take(hd, g):
                wait(dve, gram_used, 8 * hd + g)
                dve.wait_ge(gram_ps, 8 * hd + g + 1)
                nc.vector.sem_inc(taking, 1)
                mk = masks[:, g:g + 1, :]
                if g in SAMPLE_GRAM:
                    nc.vector.copy_predicated(As[:], masks[0:NS, SAMPLE_GRAM[g], 0:NS], aux[0:NS, 2, P - NS:P])
                nc.vector.copy_predicated(A[:], mk.to_broadcast([P, NCH, P]),
                                          aux[:, g % 2, :].rearrange("p (c s) -> p c s", c=NCH)).then_inc(gram_used, 1)

            def mixer(t, par, front, rec, tail):
                hd, rp, td = t - 1, 1 - par, t - 2
                b0 = 4 * t

                def new_state(c):
                    dve.wait_ge(s1_ps, 2 * td + c + 1)
                    dve.wait_ge(s0_mul, td + 1)
                    s1 = S1[:, 4 * c:4 * c + 4]
                    nc.vector.tensor_tensor(s1, s1, aux[:, 2, :].rearrange("p (n v) -> p n v", n=4), ALU.add)\
                        .then_inc(s1_ok, 1)

                if front and not (isinstance(t, int) and t == 0):
                    lo(Pos(1, t, 4))
                if rec:
                    wait(dve, gate_ok, hd)
                    scaled(gr[:], b0 - 1, 1, gr_ok)
                    dve.wait_ge(gr_ok, hd + 1)
                    nc.vector.sem_inc(evac, 1)
                    pb = b_[:, rp, 0:SEQ].rearrange("p (c s) -> p c s", c=NCH)
                    sbv = b_[:, rp, SEQ:T].rearrange("p (c s) -> p c s", c=NSEQ)
                    wait(dve, kT_ps, hd)
                    nc.vector.tensor_tensor(kd[:, 0:SEQ].rearrange("p (c s) -> p c s", c=NCH),
                                            pb[:, :, CH - 1:CH].to_broadcast([P, NCH, CH]), pb, ALU.subtract)
                    nc.vector.tensor_tensor(kd[:, SEQ:T].rearrange("p (c s) -> p c s", c=NSEQ),
                                            sbv[:, :, DSEQ - 1:DSEQ].to_broadcast([P, NSEQ, DSEQ]), sbv, ALU.subtract)\
                        .then_inc(kdd_ok, 1)
                    diff(hd, rp, 0)
                    diff(hd, rp, 1)
                    logsig(gr, gl, g_t, gl_ok, hd)
                    dve.wait_ge(kde_ok, hd + 1)
                    nc.vector.tensor_tensor(kd[:], kd[:], k_[:, rp], ALU.mult).then_inc(kd_ok, 1)
                    dve.wait_ge(q_ok, hd + 1)
                    zed(hd, rp, 0)
                if tail:
                    new_state(0)
                if rec:
                    dve.wait_ge(eb_ok, hd + 1)
                    wait(dve, o_ps, hd)
                    nc.vector.tensor_tensor(qd[:], q_[:, rp], eb[:], ALU.mult).then_inc(qd_ok, 1)
                    zed(hd, rp, 1)
                    diff(hd, rp, 2)
                if tail:
                    dve.wait_ge(orr_ok, td + 1)
                    g = gains[:, G_ON:G_ON + 1]
                    nc.vector.scalar_tensor_tensor(out=og[:, 0:SEQ], in0=aux[:, 0, :], scalar=g, in1=orr[:, 0:SEQ],
                                                   op0=ALU.mult, op1=ALU.mult).then_inc(og_ok, 1)
                    nc.vector.scalar_tensor_tensor(out=og[:, SEQ:T], in0=aux[:, 1, 0:NS], scalar=g, in1=orr[:, SEQ:T],
                                                   op0=ALU.mult, op1=ALU.mult).then_inc(og_ok, 1)
                    dve.wait_ge(og_ok, 2 * td + 2)
                    dve.wait_ge(gate_ok, td + 1)
                    nc.vector.tensor_tensor(og[:], og[:], gate[:], ALU.mult).then_inc(ogg_ok, 1)
                if front:
                    wait(dve, k_ok, t)
                    scaled(fr[:], b0, 0, fr_ok)
                    dve.wait_ge(fr_ok, t + 1)
                    nc.vector.sem_inc(evac, 1)
                    lo(Pos(2, t, 4))
                if tail:
                    new_state(1)
                    dve.wait_ge(oh_ok, td + 1)
                    nc.vector.tensor_tensor(tile_of(ol, td), og[:], tile_of(oh, td).bitcast(F32), ALU.subtract)\
                        .then_inc(ol_ok, 1)
                if rec:
                    take(hd, 0)
                if front:
                    logsig(fr, fl, f_t, lf_ok, t)
                    dve.wait_ge(lf_ok, t + 1)
                    nc.vector.tensor_tensor_scan(b_[:, par, :], keep[:], fl[:], 0.0, ALU.mult, ALU.add).then_inc(b_ok, 1)
                if rec:
                    take(hd, 1)
                    zed(hd, rp, 2)
                    diff(hd, rp, 3)
                if front:
                    wait(dve, q_ok, t)
                    scaled(qr[:], b0 + 1, 1, qr_ok)
                    dve.wait_ge(qr_ok, t + 1)
                    nc.vector.sem_inc(evac, 1)
                if rec:
                    take(hd, 2)
                if front:
                    lo(Pos(3, t, 4))
                if rec:
                    zed(hd, rp, 3)
                    diff(hd, rp, 4)
                    take(hd, 3)
                if front:
                    logsig(qr, ql, q_t, ql_ok, t)
                if rec:
                    zed(hd, rp, 4)
                    diff(hd, rp, 5)
                if front:
                    wait(dve, vT_ps, t)
                    scaled(vT[:], b0 + 2, 0, vT_ok)
                    dve.wait_ge(vT_ok, t + 1)
                    nc.vector.sem_inc(evac, 1)
                if rec:
                    take(hd, 4)
                    zed(hd, rp, 5)
                    diff(hd, rp, 6)
                if front:
                    lo(Pos(4, t, 4))
                if rec:
                    take(hd, 5)
                    zed(hd, rp, 6)
                    take(hd, 6)
                    dve.wait_ge(ds_ps, hd + 1)
                    wait(dve, s_out, 16 * hd)
                    dv = aux[:, 3, :].rearrange("p (c v) -> p c v", c=NCH)
                    nc.vector.tensor_copy(S[:, 0], dv[:, 0]).then_inc(s_step, 1)
                    for c in range(1, NCH):
                        dve.wait_ge(s_step, 4 * hd + c)
                        nc.vector.scalar_tensor_tensor(out=S[:, c], in0=S[:, c - 1],
                                                       scalar=eb[:, CH * c + CH - 1:CH * c + CH],
                                                       in1=dv[:, c], op0=ALU.mult, op1=ALU.add).then_inc(s_step, 1)
                    take(hd, 7)

            nc.vector.memset(eps[:], EPS).then_inc(setup, 1)
            nc.vector.memset(A[:], 0.0)
            nc.vector.memset(As[:], 0.0)
            nc.vector.memset(kTs[NS:P, :], 0.0)
            nc.vector.memset(Vb[NS:P], 0.0)
            dve.wait_ge(ld_gain, 16)
            for m in range(DT):
                gain_lo(xl, xh, m, G_MIX, m)
                if m == 0:
                    lo(Pos(0))
                if m == 6:
                    lo(Pos(1))
            dve.wait_ge(rms_done, 1)
            dve.wait_ge(ld_const, 80)
            dve.wait_ge(ld_mask, 16)
            nc.vector.tensor_copy(masks[:].rearrange("p a n -> p (a n)"), Z[:].rearrange("p a n -> p (a n)")[:, 0:8 * P])\
                .then_inc(setup, 1)
            dve.wait_ge(setup, 2)
            mixer(0, 0, True, False, False)
            mixer(1, 1, True, True, False)
            with dve.Fori(1, 4) as i:
                mixer(2 * i, 0, True, True, True)
                mixer(2 * i + 1, 1, True, True, True)
            mixer(8, 0, False, True, True)
            mixer(9, 1, False, False, True)

            def add_h(m, b, tp, n_h):
                dve.wait_ge(block_done, b + 1)
                nc.vector.tensor_tensor(halves(tile_of(h, m)), halves(tile_of(h, m)), acc[:, tp, :, 0:HALF], ALU.add)\
                    .then_inc(h_ok, 1)
                dve.wait_ge(h_ok, n_h)
                nc.vector.sem_inc(evac, 1)

            def ffn(layer, b_in, b_out, g_next, n_norm, h_base, x_base, t_in, t_out):
                for m in range(DT):
                    if m or layer == 0:
                        lo(Pos(b_in - 8 + m + 1))
                    add_h(m, b_in - 8 + m, (t_in - 8 + m) % 2, h_base + m + 1)
                    gain_lo(xl, xh, m, G_FFN + 8 * layer, x_base + m)
                lo(Pos(b_in + 1))
                dve.wait_ge(rms_done, n_norm + 1)
                dve.wait_ge(s_out, 16 * HEADS)
                dve.wait_ge(s1_out, 16 * HEADS)
                nc.vector.memset(u[:, 0:2], 0.0)
                def pair(k, i):
                    f = 2 * i + k
                    n = FT * layer + f
                    b = b_in + 2 * f
                    tp = (t_in) % 2
                    dve.wait_ge(block_done, b + 1)
                    wait(dve, cst_ok, 2 * n)
                    wait(dve, c2_ok, 2 * n)
                    nc.vector.tensor_tensor(u[:, 2:2 + HALF], acc[:, tp, 0, 0:HALF], rms[:, 0:HALF], ALU.mult)
                    nc.vector.tensor_tensor(u[:, 2 + HALF:2 + SEQ], acc[:, tp, 1, 0:SEQ - HALF], rms[:, HALF:SEQ], ALU.mult)
                    us = u[:, 2 + SEQ:UW].rearrange("p (n t) -> p n t", n=NSEQ)
                    nc.vector.tensor_tensor(us[:, :, 2:], acc[:, tp, 1, SEQ - HALF:HALF].rearrange("p (n t) -> p n t", n=NSEQ),
                                            rms[:, SEQ:T].rearrange("p (n t) -> p n t", n=NSEQ), ALU.mult).then_inc(u_ok, 1)
                    dve.wait_ge(u_ok, n + 1)
                    nc.vector.sem_inc(evac, 1)
                    lo(Pos(b_in + 2 * k + 2, i, 4))
                    cw = G_CW + 3 * FT * layer
                    dve.wait_ge(c0_ok, 2 * n + 2)
                    dve.wait_ge(ubuf_ok, n + 1)
                    at = a_[:, SEQ:T].rearrange("p (n t) -> p n t", n=NSEQ)
                    for j in (1, 0):
                        w = col_of(gains, cw + FT * j + f)
                        nc.vector.scalar_tensor_tensor(out=a_[:, 0:SEQ], in0=u[:, j:j + SEQ], scalar=w, in1=a_[:, 0:SEQ],
                                                       op0=ALU.mult, op1=ALU.add)
                        nc.vector.scalar_tensor_tensor(out=at, in0=us[:, :, j:j + DSEQ], scalar=w, in1=at,
                                                       op0=ALU.mult, op1=ALU.add).then_inc(c2_ok, 1)
                        if j == 1:
                            dve.wait_ge(c2_ok, 2 * n + 1)
                    lo(Pos(b_in + 2 * k + 3, i, 4))
                    dve.wait_ge(silr_ok, n + 1)
                    dve.wait_ge(block_done, b + 2)
                    nc.vector.tensor_tensor(halves(sil[:]), acc[:, 1 - tp, :, 0:HALF], halves(sil[:]), ALU.mult).then_inc(prod_ok, 1)
                    dve.wait_ge(prod_ok, n + 1)
                    nc.vector.sem_inc(evac, 1)
                    dve.wait_ge(gh_ok, n + 1)
                    nc.vector.tensor_tensor(tile_of(glo, f), sil[:], tile_of(gh, f).bitcast(F32), ALU.subtract).then_inc(glo_ok, 1)
                pair(0, 0)
                pair(1, 0)
                with dve.Fori(1, FT // 2) as i:
                    pair(0, i)
                    pair(1, i)
                def body(i, last):
                    for m4 in range(4):
                        for c in range(3):
                            if not (last and m4 == 3 and c == 2) and not (isinstance(i, int) and i == m4 == c == 0):
                                nxt = (c + 1) % 3
                                lo(Pos(b_out + 3 * m4 + c + 1, i, 12), 128 * len(FO_K[nxt]) if not (m4 == 3 and c == 2) else 1024)
                        m = 4 * i + m4
                        add_h(m, b_out + 3 * m + 2, (t_out + m4) % 2, h_base + 8 + m + 1)
                        if g_next is not None:
                            gain_lo(xl, xh, m, g_next, x_base + 8 + m)
                body(0, False)
                body(1, g_next is None)
            ffn(0, B_FI0, B_FO0, G_KV, 1, 0, 8, T_FI0, T_FO0)
            def key_raw(dst, p, n, b, tp):
                scaled(tile_of(dst, p), b, tp, kr_ok)
                dve.wait_ge(kr_ok, n + 1)
                nc.vector.sem_inc(evac, 1)

            def key_gain(dst, p, n, g):
                dve.wait_ge(krk_ok, n + 1)
                nc.vector.scalar_tensor_tensor(out=tile_of(dst, p), in0=tile_of(dst, p), scalar=g, in1=sq[:],
                                               op0=ALU.mult, op1=ALU.mult).then_inc(kn_ok, 1)

            lo(Pos(B_KV + 1))
            dve.wait_ge(rms_done, 3)
            dve.wait_ge(block_done, B_KV + 1)
            dve.wait_ge(ld_kv, 64)
            nc.vector.tensor_scalar(gq[:], gains[:, G_Q:G_Q + 1], 0.125, None, ALU.mult).then_inc(gq_ok, 1)
            nc.vector.memset(Vst[:], 0.0).then_inc(z_set, 1)
            nc.vector.tensor_tensor(halves(fx[:]), acc[0:FOX, T_KV % 2, :, 0:HALF], halves(rms[0:FOX, :]), ALU.mult).then_inc(fx_ok, 1)
            dve.wait_ge(fx_ok, 1)
            nc.vector.sem_inc(evac, 1)
            nc.vector.tensor_scalar(fx[:], fx[:], gains[0:FOX, G_BF:G_BF + 1], None, ALU.add).then_inc(fb_ok, 1)
            lo(Pos(B_KV + 2))
            dve.wait_ge(fe_t, 3)
            nc.vector.scalar_tensor_tensor(out=fx[:], in0=fx[:], scalar=0.0, in1=fe[:], op0=ALU.min, op1=ALU.subtract)\
                .then_inc(flf_ok, 1)
            dve.wait_ge(flf_ok, 1)
            nc.vector.tensor_tensor_scan(c16[:], keep_c[0:FOX, :], fx[:], 0.0, ALU.mult, ALU.add).then_inc(c16_ok, 1)
            dve.wait_ge(c16_ok, 1)
            nc.vector.tensor_copy(c16h[:], c16[:]).then_inc(ch_ok, 1)
            dve.wait_ge(ch_ok, 1)
            nc.vector.tensor_tensor(c16l[:], c16[:], c16h[:].bitcast(F32), ALU.subtract).then_inc(cl_ok, 1)
            def kv_pair(k, p, i, step, first):
                b = B_KV + 1 + 2 * p
                if not first:
                    lo(Pos(B_KV + 2 + 2 * k, i, step))
                key_raw(KT, p, p, b, (T_KV + 1) % 2)
                gain_lo(x2l, x2h, p, G_MIX + DT, 24 + p)
                lo(Pos(B_KV + 3 + 2 * k, i, step))
                if not (isinstance(p, int) and p < 2):
                    dve.wait_ge(v_out[k], 16 * (i if k == 0 else i))
                scaled(vT2[:, k, :], b + 1, T_KV % 2, v2_ok)
                dve.wait_ge(v2_ok, p + 1)
                nc.vector.sem_inc(evac, 1)
                key_gain(KT, p, p, gains[:, G_K:G_K + 1])
            kv_pair(0, 0, 0, 4, True)
            dve.wait_ge(rep_ps, 1)
            nc.vector.tensor_copy(C[:, SEQ:T], aux[:, 2, 0:NS]).then_inc(c_ok, 1)
            kv_pair(1, 1, 0, 4, False)
            with dve.Fori(1, 4) as i:
                kv_pair(0, 2 * i, i, 4, False)
                kv_pair(1, 2 * i + 1, i, 4, False)
            dve.wait_ge(cl_in, 16 * NSEQ * PAGES)
            nc.vector.tensor_tensor_scan(C[:, 0:SEQ], keep_c[:, 0:SEQ], CL[:], 0.0, ALU.mult, ALU.add).then_inc(c_scan, 1)
            dve.wait_ge(c_scan, 1)
            nc.vector.tensor_scalar(C[:, SEQ:T], C[:, SEQ:T], C[:, SEQ - 1:SEQ], None, ALU.add).then_inc(c_ok, 1)
            dve.wait_ge(gq_ok, 1)

            def qg_pair(k, p, i, step):
                b = B_QG + 2 * p
                if isinstance(p, int) and p == 0:
                    lo(Pos(B_QG + 1))
                    dve.wait_ge(c_dram, 32)
                    dve.wait_ge(v_out[0], 64)
                    dve.wait_ge(v_out[1], 64)
                    dve.wait_ge(f_out, 16)
                    dve.wait_ge(v2_ps, 8)
                    dve.wait_ge(c_ok, 2)
                key_raw(QT, p, p + 8, b, T_QG % 2)
                lo(Pos(B_QG + 2 + 2 * k, i, step))
                scaled(tile_of(GT, p), b + 1, (T_QG + 1) % 2, gx_ok)
                dve.wait_ge(gx_ok, p + 1)
                nc.vector.sem_inc(evac, 1)
                lo(Pos(B_QG + 3 + 2 * k, i, step))
                key_gain(QT, p, p + 8, gq[:, 0:1])
                dve.wait_ge(gx_t, 3 * p + 3)
                g = tile_of(GT, p)
                nc.vector.scalar_tensor_tensor(out=g, in0=g, scalar=0.0, in1=gate_log[:], op0=ALU.min, op1=ALU.subtract)\
                    .then_inc(gx_ls, 1)
            qg_pair(0, 0, 0, 4)
            qg_pair(1, 1, 0, 4)
            with dve.Fori(1, 4) as i:
                qg_pair(0, 2 * i, i, 4)
                qg_pair(1, 2 * i + 1, i, 4)

            def att(i, cur, prev):
                def mx(x):
                    n = 8 * i + x
                    w = P * (x % 4 + 1)
                    dve.wait_ge(sc_ps, n + 1)
                    nc.vector.tensor_reduce(nm[:, x:x + 1], S_ps(x % 2)[:, 0:w], AX.X, ALU.max, negate=True).then_inc(mx_ok, 1)

                def over(x):
                    n = 8 * i + x
                    a, tb = (x % 8) // 4, x % 4
                    dve.wait_ge(ex_ok, n + 1)
                    nc.vector.reciprocal(rr[:, x % 8:x % 8 + 1], rs[:, x % 8:x % 8 + 1]).then_inc(rc_ok, 1)
                    dve.wait_ge(pv_ps, n + 1)
                    if x == 0:
                        wait(dve, u_ps, i)
                    dve.wait_ge(rc_ok, n + 1)
                    nc.vector.tensor_scalar(OT[:, tb, 64 * a:64 * a + 64], O_ps[:, 64 * a:64 * a + 64],
                                            rr[:, x % 8:x % 8 + 1], None, ALU.mult).then_inc(ov_ok, 1)

                def diagonal(hf):
                    dve.wait_ge(dpv_ps, 2 * i - 1 + hf)
                    for a in range(2):
                        r, o = slice(64 * a, 64 * a + 64), 64 * hf + 8 * a
                        g = GT[r, 4 * hf:4 * hf + 4, bass.ds(SEQ + DSEQ * (i - 1), DSEQ)]
                        nc.vector.tensor_tensor(g[:, 0:3, :], O2_ps[r, 0:3 * 144].rearrange("p (k c) -> p k c", c=144)[:, :, o:o + 8],
                                                g[:, 0:3, :], ALU.mult)
                        last = nc.vector.tensor_tensor(g[:, 3, :], O2_ps[r, 3 * 144 + o:3 * 144 + o + 8], g[:, 3, :], ALU.mult)
                    last.then_inc(dgo_ok, 1)

                if prev:
                    dve.wait_ge(d_ps, i)
                    nc.vector.tensor_reduce(dm[:, 0:1], D_ps[:, :, 0:HALF], AX.XY, ALU.max, negate=True).then_inc(dmx_ok, 1)
                if cur:
                    mx(0)
                if prev:
                    over(-2)
                    dve.wait_ge(dex_ok, i)
                    nc.vector.reciprocal(dm[:, 2:3], dm[:, 1:2]).then_inc(drc_ok, 1)
                    dve.wait_ge(drc_ok, i)
                    nc.vector.tensor_scalar(Pd[:], Pd[:], dm[:, 2:3], None, ALU.mult).then_inc(dpn_ok, 1)
                if cur:
                    mx(1)
                if prev:
                    over(-1)
                if cur:
                    nc.vector.tensor_scalar(cc[:], C[:], col_of(seq_col, i), None, ALU.mult).then_inc(cc_ok, 1)
                    mx(2)
                if prev:
                    dve.wait_ge(u_ps, i)
                    g = tile_of(GT, i - 1)[:, 0:SEQ]
                    nc.vector.tensor_tensor(g, U_ps, g, ALU.mult).then_inc(go_ok, 1)
                if cur:
                    over(0)
                if prev:
                    diagonal(0)
                if cur:
                    mx(3)
                    over(1)
                    mx(4)
                    over(2)
                if prev:
                    diagonal(1)
                if cur:
                    for x in range(5, 8):
                        mx(x)
                        over(x - 2)
            dve.wait_ge(block_done, B_WO1)
            dve.wait_ge(ld_mask, 48)
            nc.vector.tensor_copy(bfc[:], wide[:, 0:2 * P + NSEQ * NS]).then_inc(zero_ok, 1)
            nc.vector.tensor_copy(sel[:].rearrange("p a n -> p (a n)"), wide[0:4, 2 * P + NSEQ * NS:]).then_inc(zero_ok, 1)
            nc.vector.memset(Qb[:], 0.0).then_inc(zero_ok, 1)
            dve.wait_ge(gt_ok, 8)
            att(0, True, False)
            att(1, True, True)
            with dve.Fori(1, 4) as i:
                att(2 * i, True, True)
                att(2 * i + 1, True, True)
            att(8, False, True)
            for p in range(DT):
                dve.wait_ge(ah_ok, p + 1)
                nc.vector.tensor_tensor(al[:, p, :], GT[:, p, :], ah[:, p, :].bitcast(F32), ALU.subtract).then_inc(al_ok, 1)
            ffn(1, B_FI1, B_FO1, None, 3, 16, 32, T_FI1, T_FO1)

        @block.gpsimd
        def _(pool):
            def add_square(n, src=sq):
                pool.wait_ge(sq_done, n + 1)
                nc.gpsimd.tensor_tensor(ssq[:], ssq[:], src[:], ALU.add).then_inc(ssq_done, 1)

            def first_square(n):
                pool.wait_ge(sq_done, n + 1)
                nc.gpsimd.sem_inc(ssq_done, 1)

            first_square(0)
            for m in range(1, DT):
                if m > 1:
                    pool.wait_ge(ssq_done, m)
                add_square(m, (sq, rms)[1 - m % 2])

            def mixer(t, par, front, rec, tail):
                hd, td = t - 1, t - 2
                if rec and tail:
                    pool.wait_ge(ld_const, 80)
                    pool.wait_ge(s0_mul, td + 1)
                    pool.wait_ge(o_ps, td + 1)
                    pool.dma_start(S0[:].rearrange("p n v -> p (n v)"), row_of(d["s0"], hd)).then_inc(s0_in, 16)
                if rec:
                    pool.wait_ge(g_sig, hd + 1)
                    wait(pool, ogg_ok, hd)
                    nc.gpsimd.tensor_tensor(gate[:], gr[:], gl[:], ALU.mult).then_inc(gate_ok, 1)
                if front:
                    pool.wait_ge(lf_ok, t + 1)
                    nc.gpsimd.tensor_tensor(kd0[:], fl[:], fr[:], ALU.subtract).then_inc(kd0_ok, 1)
                if tail:
                    pool.wait_ge(s_step, 4 * td + 4)
                    pool.dma_start(row_of(d["hgrn_p"], td), S[:, NCH - 1]).then_inc(s_out, 16)
                    pool.wait_ge(ld_const, 80)
                    pool.wait_ge(s1_ok, 2 * td + 2)
                    pool.dma_start(row_of(d["hgrn_s"], td), S1[:].rearrange("p n v -> p (n v)")).then_inc(s1_out, 16)
                if rec:
                    pool.wait_ge(s0_in, 16 * hd + 16)
                    pool.wait_ge(eb_ok, hd + 1)
                    wait(pool, s1_out, 16 * hd)
                    e = eb[:, SEQ:T].rearrange("p (n t) -> p n t", n=NSEQ)[:, :, DSEQ - 1:DSEQ]
                    nc.gpsimd.tensor_tensor(S1[:], S0[:], e.to_broadcast([P, NSEQ, P]), ALU.mult).then_inc(s0_mul, 1)
                if front:
                    pool.wait_ge(q_sig, t + 1)
                    nc.gpsimd.tensor_tensor(q_[:, par], qr[:], ql[:], ALU.mult).then_inc(q_ok, 1)
                if rec:
                    pool.wait_ge(v_ok, 2 * hd + 2)
                    wait(pool, s1_ps, 2 * hd)
                    nc.gpsimd.tensor_tensor(Vb[0:NS], Vs[:].unsqueeze(1).to_broadcast([NS, NSEQ, P]),
                                            blk[0:NS, :].unsqueeze(2).to_broadcast([NS, NSEQ, P]), ALU.mult).then_inc(vb_ok, 1)
            pool.dma_start(S0[:].rearrange("p n v -> p (n v)"), d["s0"][0]).then_inc(s0_in, 16)
            pool.wait_ge(ld_const, 80)
            mixer(0, 0, True, False, False)
            mixer(1, 1, True, True, False)
            with pool.Fori(1, 4) as i:
                mixer(2 * i, 0, True, True, True)
                mixer(2 * i + 1, 1, True, True, True)
            mixer(8, 0, False, True, True)
            mixer(9, 1, False, False, True)

            def squares(s_base):
                first_square(s_base)
                pool.wait_ge(ssq_done, s_base + 1)
                add_square(s_base + 1)
                with pool.Fori(2, DT) as m:
                    pool.wait_ge(ssq_done, s_base + m)
                    add_square(s_base + m)

            def ffn(layer, b_in, has_next, s_base):
                squares(s_base)
                pool.wait_ge(x_lo, s_base + 8 * layer + 8)
                pool.wait_ge(s_out, 16 * HEADS)
                pool.wait_ge(s1_out, 16 * HEADS)
                wait(pool, out_cst, 16 * layer)
                pool.dma_start(cin[:], d["conv_in"][layer]).then_inc(st_in, 16)
                pool.wait_ge(st_in, 16 * layer + 16)
                def pair(f):
                    n = FT * layer + f
                    us = u[:, 2 + SEQ:UW].rearrange("p (n t) -> p n t", n=NSEQ)
                    ci = cin[:, bass.ds(16 * f, 16)].rearrange("p (n t) -> p n t", n=NSEQ)
                    wait(pool, c2_ok, 2 * n)
                    nc.gpsimd.tensor_copy(us[:, :, 0:2], ci).then_inc(ubuf_ok, 1)
                    pool.wait_ge(u_ok, n + 1)
                    nc.gpsimd.tensor_copy(cst[:, bass.ds(18 * f, 2)], u[:, SEQ:SEQ + 2]).then_inc(cst_ok, 1)
                    nc.gpsimd.tensor_copy(cst[:, bass.ds(18 * f + 2, 16)].rearrange("p (n t) -> p n t", n=NSEQ),
                                          us[:, :, DSEQ:DSEQ + 2]).then_inc(cst_ok, 1)
                    pool.wait_ge(sil_ok, n + 1)
                    nc.gpsimd.tensor_tensor(sil[:], sil[:], rms[:], ALU.mult).then_inc(silr_ok, 1)
                pair(0)
                with pool.Fori(1, FT) as f:
                    pair(f)
                pool.wait_ge(cst_ok, 2 * FT * (layer + 1))
                pool.dma_start(d["conv_out"][layer], cst[:]).then_inc(out_cst, 16)
                if has_next:
                    squares(s_base + 8)
            ffn(0, B_FI0, True, 8)
            pool.wait_ge(flf_ok, 1)
            pool.dma_start(d["f_out"], fx[:]).then_inc(f_out, 16)
            pool.wait_ge(cl_ok, 1)
            for e, part in enumerate((c16h, c16l)):
                pool.dma_start(d["c_row"][:, e, :], part[:, 0:SEQ]).then_inc(c_dram, 16)

            def kv_pair(k, p):
                pool.wait_ge(v2_ok, p + 1)
                pool.dma_start(row_of(d["v_out"], p), vT2[:, k, :]).then_inc(v_out[k], 16)
                pool.wait_ge(kn_ok, p + 1)
                pool.dma_start(row_of(d["k_out"], p), tile_of(KT, p)).then_inc(k_out[k], 16)
            with pool.Fori(0, 4) as i:
                kv_pair(0, 2 * i)
                kv_pair(1, 2 * i + 1)

            pool.wait_ge(block_done, B_QG)
            nc.gpsimd.tensor_copy(Kd[:, :, SEQ:T], KT[:, :, SEQ:T]).then_inc(kn_in, 1)
            pool.wait_ge(block_done, B_WO1)
            pool.wait_ge(c_dram, 32)
            pool.wait_ge(kn_in, 1)
            nc.gpsimd.memset(QX[:, 0], 0.0).then_inc(kn_in, 1)

            def queries(k, i):
                wait(pool, sc_ps, 8 * (i - 1))
                pool.dma_start(cX[:, k, :], d["c_row"][bass.ds(2 * i, 2)].rearrange("h e n -> (h e) n")).then_inc(cx_in[k], 16)
                if isinstance(i, int) and i == 0:
                    pool.wait_ge(kn_ok, 9)
                    pool.wait_ge(kn_in, 2)
                for a in range(2):
                    r = slice(64 * a, 64 * a + 64)
                    wait(pool, qx_ok, 2 * i + a)
                    nc.gpsimd.tensor_copy(QX[r, k, a, :], QT[r, bass.ds(i, 1), 0:SEQ].rearrange("p a n -> p (a n)"))\
                        .then_inc(qx_ok, 1)

            def sample_queries(i):
                wait(pool, d_ps, i)
                for a in range(2):
                    r = slice(64 * a, 64 * a + 64)
                    wait(pool, qx_ok, 2 * i + 2)
                    wait(pool, qb_ok, 2 * i + a)
                    nc.gpsimd.tensor_copy(Qb[r, :].rearrange("p (k c) -> p k c", c=144)[:, :, 8 * a:8 * a + 8],
                                          QT[r, :, bass.ds(SEQ + DSEQ * i, DSEQ)]).then_inc(qb_ok, 1)
            queries(0, 0)
            pool.wait_ge(zero_ok, 3)
            sample_queries(0)
            pool.wait_ge(qb_ok, 2)
            nc.gpsimd.memset(QX[:, 1], 0.0).then_inc(zero_ok, 1)
            pool.wait_ge(zero_ok, 4)
            nc.gpsimd.memset(PTd[:], 0.0).then_inc(zero_ok, 1)
            pool.wait_ge(zero_ok, 5)
            queries(1, 1)
            sample_queries(1)
            with pool.Fori(1, 4) as i:
                for k in range(2):
                    queries(k, 2 * i + k)
                    sample_queries(2 * i + k)
            ffn(1, B_FI1, False, 24)
            for m in range(DT):
                pool.wait_ge(h_ok, 24 + m + 1)
                pool.dma_start(d["y"][m], h[:, m, :]).then_inc(y_out, 16)
            pool.wait_ge(y_out, 16 * DT)
            pool.wait_ge(out_cst, 32)
            pool.wait_ge(f_out, 16)
            for k in range(2):
                pool.wait_ge(k_out[k], 64)
                pool.wait_ge(v_out[k], 64)

        @block.tensor
        def _(pe):
            def gemm(pos, tile, tp, kts, rh, rl, first=True, last=True, wait_x=None, mid=None):
                pe.wait_ge(lo_done, pos.b + 1)
                if first:
                    wait(pe, evac, tile - 1)
                sp_ = pos.slot % SPL
                for j, kt in enumerate(kts):
                    if wait_x is not None:
                        pe.wait_ge(wait_x[0], wait_x[1] + kt + 1)
                    for n, (W, X) in enumerate(((w_hi, rl), (w_lo, rh), (w_hi, rh))):
                        for hf in range(2):
                            mm = nc.tensor.matmul(acc[:, tp, hf, 0:HALF], W[:, sp_, 128 * j:128 * j + 128],
                                                  X[:, kt, HALF * hf:HALF * hf + HALF],
                                                  start=(first and j == 0 and n == 0),
                                                  stop=(last and j == len(kts) - 1 and n == 2))
                    if mid is not None and j in mid:
                        mid[j]()
                mm.then_inc(block_done, 1)

            def norm(n, n_ssq):
                pe.wait_ge(ssq_done, n_ssq)
                for hf in range(2):
                    mm = nc.tensor.matmul(aux[:, hf, 0:HALF], mean_all[:], ssq[:, HALF * hf:HALF * hf + HALF],
                                          start=True, stop=True)
                mm.then_inc(norm_ps, 1)

            def gram(hd, rp, g):
                if g == 0:
                    pe.wait_ge(k_ok, hd + 1)
                    pe.wait_ge(q_ok, hd + 1)
                    lhs, rhs = k_[:, rp], q_[:, rp]
                else:
                    pe.wait_ge(z_ok, 7 * hd + g)
                    lhs = rhs = Z[:, (g - 1) % 2]
                wait(pe, gram_used, 8 * hd + g - 1)
                for c in range(NCH):
                    mm = nc.tensor.matmul(aux[:, g % 2, CH * c:CH * c + CH], lhs[:, CH * c:CH * c + CH],
                                          rhs[:, CH * c:CH * c + CH], start=True, stop=True)
                if g in SAMPLE_GRAM:
                    if g == 3:
                        pe.wait_ge(kT_ok, 2 * hd + 2)
                        lhs, rhs = k_[:, rp], q_[:, rp]
                    elif g > 5:
                        pe.wait_ge(gram_used, 8 * hd + g)
                    mm = nc.tensor.matmul(aux[0:NS, 2, 0:P], lhs[:, SEQ:T], rhs[:, T - P:T], start=True, stop=True)
                mm.then_inc(gram_ps, 1)

            def turn(src):
                for c in range(NCH):
                    nc.tensor.transpose(aux[:, 3, CH * c:CH * c + CH], src[:, CH * c:CH * c + CH], ident[:])
                return nc.tensor.transpose(aux[0:NS, 2, 0:P], src[:, SEQ:T], ident[:])

            def mixer(t, par, front, rec, tail):
                hd, rp, td = t - 1, 1 - par, t - 2

                def turn_v():
                    pe.wait_ge(vT_ok, hd + 1)
                    wait(pe, orr_ok, hd)
                    wait(pe, s1_ok, 2 * hd)
                    turn(vT).then_inc(vT_ps, 1)

                def turn_k():
                    pe.wait_ge(kd_ok, hd + 1)
                    pe.wait_ge(v_ok, 2 * hd + 2)
                    turn(kd).then_inc(kT_ps, 1)

                def gram_0():
                    wait(pe, og_ok, 2 * hd)
                    gram(hd, rp, 0)

                def ds():
                    pe.wait_ge(kT_ok, 2 * hd + 2)
                    for c in range(NCH):
                        mm = nc.tensor.matmul(aux[:, 3, CH * c:CH * c + CH], kT[:, c], V[:, c], start=True, stop=True)
                    mm.then_inc(ds_ps, 1)

                def outs():
                    pe.wait_ge(gram_used, 8 * td + 8)
                    pe.wait_ge(s_step, 4 * td + 3)
                    pe.wait_ge(s0_in, 16 * td + 16)
                    pe.wait_ge(qd_ok, td + 1)
                    for c in range(NCH):
                        o = aux[:, 0, CH * c:CH * c + CH]
                        nc.tensor.matmul(o, V[:, c], A[:, c], start=True, stop=(c == 0))
                        if c:
                            nc.tensor.matmul(o, S[:, c - 1], qd[:, CH * c:CH * c + CH], start=False, stop=True)
                    o = aux[:, 1, 0:NS]
                    for n in range(NSEQ):
                        nc.tensor.matmul(o[:, DSEQ * n:DSEQ * n + DSEQ], S0[:, n], qd[:, SEQ + DSEQ * n:SEQ + DSEQ * (n + 1)],
                                         start=(n == 0), stop=False)
                    nc.tensor.matmul(o, Vs[:], As[:], start=False, stop=True).then_inc(o_ps, 1)

                def state(c):
                    pe.wait_ge(vb_ok, td + 1)
                    wait(pe, s1_ok, 2 * td + c) if c else None
                    nc.tensor.matmul(aux[:, 2, :], kTs[:], Vb[:, 4 * c:4 * c + 4, :], start=True, stop=True).then_inc(s1_ps, 1)

                def onorm():
                    pe.wait_ge(s_step, 4 * td + 4)
                    pe.wait_ge(osq_ok, 2 * td + 2)
                    nc.tensor.matmul(aux[:, 3, :], mean_head[:], osq[:, 0:SEQ], start=True, stop=True)
                    nc.tensor.matmul(aux[:, 1, 64:64 + NS], mean_head[:], osq[:, SEQ:T], start=True, stop=True).then_inc(on_ps, 1)

                quarters = (
                    {1: [(tail, outs), (tail, lambda: state(0))], 5: [(tail, onorm)]},
                    {0: [(tail, lambda: state(1))], 3: [(rec, gram_0)], 6: [(rec, lambda: gram(hd, rp, 1))]},
                    {0: [(rec, turn_v)], 2: [(rec, lambda: gram(hd, rp, 2))], 5: [(rec, turn_k)],
                     7: [(rec, lambda: gram(hd, rp, 3))]},
                    {1: [(rec, lambda: gram(hd, rp, 4))], 3: [(rec, ds)], 4: [(rec, lambda: gram(hd, rp, 5))],
                     6: [(rec, lambda: gram(hd, rp, 6))]})

                def run(steps):
                    for on, step in steps:
                        if on:
                            step()
                for k, mid in enumerate(quarters):
                    if front:
                        gemm(Pos(k, t, 4), 4 * t + k, k % 2, range(DT), xh, xl,
                             mid={j: (lambda steps=steps: run(steps)) for j, steps in mid.items()})
                    else:
                        for steps in mid.values():
                            run(steps)
                if rec:
                    gram(hd, rp, 7)

            gemm(Pos(0), 0, 0, range(DT), xh, xl, wait_x=(x_lo, 0))
            gemm(Pos(1), 1, 1, range(DT), xh, xl)
            pe.wait_ge(ld_const, 80)
            norm(0, DT)
            for k in range(2, 4):
                gemm(Pos(k), k, k % 2, range(DT), xh, xl)
            mixer(1, 1, True, True, False)
            with pe.Fori(1, 4) as i:
                mixer(2 * i, 0, True, True, True)
                mixer(2 * i + 1, 1, True, True, True)
            mixer(8, 0, False, True, True)
            mixer(9, 1, False, False, True)

            def ffn(layer, b_in, b_out, t_in, t_out, x_base, n_norm, n_ssq, rh, rl, wait_first):
                for m in range(DT):
                    gemm(Pos(b_in - 8 + m), t_in - 8 + m, (t_in + m) % 2, range(DT), rh, rl,
                         wait_x=wait_first if m == 0 else None)
                gemm(Pos(b_in), t_in, t_in % 2, range(DT), xh, xl, wait_x=(x_lo, x_base))
                norm(n_norm, n_ssq)
                gemm(Pos(b_in + 1), t_in + 1, (t_in + 1) % 2, range(DT), xh, xl)
                for k in (2, 3):
                    gemm(Pos(b_in + k), t_in + k, (t_in + k) % 2, range(DT), xh, xl)
                with pe.Fori(1, FT // 2) as i:
                    for k in range(4):
                        gemm(Pos(b_in + k, i, 4), t_in + 4 * i + k, (t_in + k) % 2, range(DT), xh, xl)
                with pe.Fori(0, 2) as i:
                    for m in range(4):
                        for c, kts in enumerate(FO_K):
                            if m == 0:
                                pe.wait_ge(glo_ok, FT * layer + kts[-1] + 1)
                            gemm(Pos(b_out + 3 * m + c, i, 12), t_out + 4 * i + m, (t_out + m) % 2, kts, gh, glo,
                                 first=(c == 0), last=(c == 2))
            ffn(0, B_FI0, B_FO0, T_FI0, T_FO0, 8, 1, 16, oh, ol, (ol_ok, 0))
            gemm(Pos(B_KV), T_KV, T_KV % 2, range(DT), xh, xl, wait_x=(x_lo, 16))
            norm(2, 24)

            def key_mean(n):
                pe.wait_ge(ksq_ok, n + 1)
                for hf in range(2):
                    mm = nc.tensor.matmul(aux[:, hf, 0:HALF], pair_mean[:], sq[:, HALF * hf:HALF * hf + HALF], start=True, stop=True)
                mm.then_inc(km_ps, 1)

            def turn_v(k, n):
                pe.wait_ge(v2_ok, n + 1)
                wait(pe, vt_ok, 2 * n)
                turn(vT2[:, k]).then_inc(v2_ps, 1)

            def kv_pair(k, p, i, step):
                gemm(Pos(B_KV + 1 + 2 * k, i, step), T_KV + 1 + 2 * p, (T_KV + 1) % 2, range(DT), xh, xl)
                if not (isinstance(p, int) and p == 0):
                    if isinstance(p, int) and p == 1:
                        pe.wait_ge(c_ok, 1)
                    turn_v(1 - k, p - 1)
                gemm(Pos(B_KV + 2 + 2 * k, i, step), T_KV + 2 + 2 * p, T_KV % 2, range(DT), xh, xl)
                if isinstance(p, int) and p == 0:
                    pe.wait_ge(ld_kv, 64)
                    pe.wait_ge(rms_done, 3)
                    pe.wait_ge(c16_ok, 1)
                    nc.tensor.matmul(aux[:, 2, 0:NS], rep16[:], c16[:, SEQ:T], start=True, stop=True).then_inc(rep_ps, 1)
                key_mean(p)
            kv_pair(0, 0, 0, 4)
            kv_pair(1, 1, 0, 4)
            with pe.Fori(1, 4) as i:
                kv_pair(0, 2 * i, i, 4)
                kv_pair(1, 2 * i + 1, i, 4)

            def qg_pair(k, p, i, step):
                first = isinstance(p, int) and p == 0
                gemm(Pos(B_QG + 2 * k, i, step), T_QG + 2 * p, T_QG % 2, range(DT), x2h, x2l, wait_x=(x_lo, 24) if first else None)
                if first:
                    turn_v(1, 7)
                gemm(Pos(B_QG + 1 + 2 * k, i, step), T_QG + 1 + 2 * p, (T_QG + 1) % 2, range(DT), x2h, x2l)
                key_mean(p + 8)
            qg_pair(0, 0, 0, 4)
            qg_pair(1, 1, 0, 4)
            with pe.Fori(1, 4) as i:
                qg_pair(0, 2 * i, i, 4)
                qg_pair(1, 2 * i + 1, i, 4)

            idb, trib = bfc[:, 0:P], bfc[:, P:2 * P]

            def att(k, i, cur, prev):
                def score(x):
                    n, a, tb = 8 * i + x, x // 4, x % 4
                    w = P * (tb + 1)
                    if not (isinstance(i, int) and n < 2):
                        pe.wait_ge(ex_ok, n - 1)
                    s = S_ps(x % 2)
                    nc.tensor.matmul(s[:, 0:w], QX[:, k, a, P * tb:P * tb + P], tile_of(KT, i)[:, 0:w], start=True, stop=False)
                    nc.tensor.matmul(s[:, w - P:w], idb, trib, start=False, stop=False)
                    nc.tensor.matmul(s[:, 0:w], sel[:, a, :], cX[:, k, 0:w], start=False, stop=True).then_inc(sc_ps, 1)

                def turn_p(x):
                    n, tb = 8 * i + x, x % 4
                    pe.wait_ge(ex_ok, n + 1)
                    wait(pe, pt_ok, n)
                    for j in range(tb + 1):
                        mm = nc.tensor.transpose(T_ps[:, P * j:P * j + P], Pr[:, x % 2, P * j:P * j + P], ident[:])
                    mm.then_inc(t_ps, 1)

                def pv(x):
                    n, tb = 8 * i + x, x % 4
                    pe.wait_ge(pt_ok, n + 1)
                    wait(pe, ov_ok, n)
                    for j in range(tb + 1):
                        at = P * i if x >= 0 else P * (i - 1)
                        mm = nc.tensor.matmul(O_ps[:, 0:P], PT[:, x % 2, j, :], Vt[:, j, bass.ds(at, P)],
                                              start=(j == 0), stop=(j == tb))
                    mm.then_inc(pv_ps, 1)

                def sample_scores(piece):
                    if piece == 0:
                        pe.wait_ge(kd_in, 64 * i + 64)
                        pe.wait_ge(qb_ok, 2 * i + 2)
                        wait(pe, dpt_ok, 2 * i)
                    if piece < 4:
                        hf = piece // 2
                        for p in range(4 * (piece % 2), 4 * (piece % 2) + 4):
                            nc.tensor.matmul(D_ps[:, hf, 0:HALF], Qb[:, P * p:P * p + P], Kd[:, p, HALF * hf:HALF * hf + HALF],
                                             start=(p == 0), stop=False)
                    else:
                        pe.wait_ge(cc_ok, i + 1)
                        for hf in range(2):
                            nc.tensor.matmul(D_ps[:, hf, 0:HALF], neg_rep[:], cc[:, HALF * hf:HALF * hf + HALF],
                                             start=False, stop=(hf == 0))
                        nc.tensor.matmul(D_ps[:, 1, HALF - NS:HALF], idb,
                                         bfc[:, bass.ds(2 * P + NS * i, NS)], start=False, stop=True).then_inc(d_ps, 1)

                def sample_out(p):
                    if p == 0:
                        pe.wait_ge(dpt_ok, 2 * i)
                        pe.wait_ge(vd_in, 64 * i)
                    if p % 4 == 0:
                        wait(pe, dgo_ok, 2 * i - 2 + p // 4)
                    o = O2_ps[:, P * (p % 4):P * (p % 4) + P]
                    for j in range(PAGES):
                        nc.tensor.matmul(o, Vd[:, j, P * p:P * p + P], PTd[:, j, :], start=(j == 0), stop=False)
                    mm = nc.tensor.matmul(o, Vst[:, P * p:P * p + P], PTd[:, PAGES, :], start=False, stop=True)
                    if p % 4 == 3:
                        mm.then_inc(dpv_ps, 1)

                if cur:
                    pe.wait_ge(qx_ok, 2 * i + 2)
                    pe.wait_ge(cx_in[k], 16 * (i // 2 + 1) if isinstance(i, int) else 8 * i + 16 - 8 * k)
                    score(0)
                if prev:
                    pv(-2)
                    turn_p(-1)
                if cur:
                    score(1)
                if prev:
                    pe.wait_ge(dpn_ok, i)
                    for j in range(PAGES):
                        nc.tensor.transpose(D_ps[:, 0, P * j:P * j + P], Pd[:, P * j:P * j + P], ident[:])
                    nc.tensor.transpose(D_ps[0:NS, 1, 0:P], Pd[:, SEQ:T], ident[:]).then_inc(dt_ps, 1)
                    pv(-1)
                if cur:
                    turn_p(0)
                if prev:
                    sample_out(0)
                    sample_out(1)
                    pe.wait_ge(ov_ok, 8 * i)
                    if not (isinstance(i, int) and i < 2):
                        pe.wait_ge(go_ok, i - 1)
                    for j in range(NCH):
                        mm = nc.tensor.transpose(U_ps[:, P * j:P * j + P], OT[:, j, :], ident[:])
                    mm.then_inc(u_ps, 1)
                if cur:
                    score(2)
                    turn_p(1)
                    pv(0)
                if prev:
                    sample_out(2)
                    sample_out(3)
                if cur:
                    score(3)
                    turn_p(2)
                    pv(1)
                    sample_scores(0)
                if prev:
                    sample_out(4)
                    sample_out(5)
                if cur:
                    score(4)
                    turn_p(3)
                    pv(2)
                if prev:
                    sample_out(6)
                    sample_out(7)
                if cur:
                    for x in range(5, 8):
                        sample_scores(x - 4)
                        score(x)
                        turn_p(x - 1)
                        pv(x - 2)
                    sample_scores(4)
            pe.wait_ge(zero_ok, 3)
            pe.wait_ge(ld_mask, 48)
            pe.wait_ge(kn_in, 2)
            pe.wait_ge(vt_ok, 16)
            pe.wait_ge(gt_ok, 8)
            att(0, 0, True, False)
            att(1, 1, True, True)
            with pe.Fori(1, 4) as i:
                att(0, 2 * i, True, True)
                att(1, 2 * i + 1, True, True)
            att(0, 8, False, True)
            ffn(1, B_FI1, B_FO1, T_FI1, T_FO1, 32, 3, 32, ah, al, (al_ok, 0))


def consts():
    import numpy as np
    c = np.zeros((P, N_CONST), np.float32)
    i = np.arange(P)
    c[:, C_ID:C_ID + P] = np.eye(P)
    c[:, C_MEAN:C_MEAN + P] = 1.0 / 1024
    c[:, C_HEAD:C_HEAD + P] = 1.0 / P
    c[:, C_PAIR:C_PAIR + P] = (i[:, None] // 64 == i[None, :] // 64) / 64.0
    c[:, C_NEG:C_NEG + P] = -1.0 * (i[:, None] % 16 == i[None, :] // 8)
    c[0:16, C_REP:C_REP + P] = (i[:16, None] == i[None, :] % 16)
    c[:, C_SEQ:C_SEQ + 8] = (i[:, None] // 16 == i[None, :8])
    c[0:NS, C_BLK:C_BLK + 8] = (i[:NS, None] // 8 == i[None, :8])
    t = np.arange(T)
    c[:, C_KEEP:C_KEEP + T] = np.where(t < SEQ, t % CH != 0, t % DSEQ != 0)
    c[:, C_KEEPC:C_KEEPC + T] = np.where(t < SEQ, t != 0, t % DSEQ != 0)
    m = np.zeros((P, 8, P), np.float32)
    m[:, 0] = np.eye(P)
    for j, w in enumerate(LEVELS):
        s, q = i[:, None], i[None, :]
        m[:, j + 1] = (s // (2 * w) == q // (2 * w)) & (s % (2 * w) < w) & (q % (2 * w) >= w)
    return c, m


def kernel(**inputs):
    import numpy as np
    import concourse.bacc as bacc
    from concourse.bass_utils import run_bass_kernel_spmd

    v = {k: np.asarray(a) for k, a in inputs.items()}

    def blocks(w):
        k, n = w.shape
        return w.reshape(k // P, P, n // P, P).transpose(2, 1, 0, 3).reshape(n // P, P, k)

    def vec(a):
        return a.reshape(-1, P).T

    n_phys = v["cache_k"].shape[0]
    x = np.concatenate([v["x_prompt"].reshape(SEQ, -1), v["x_sample"].reshape(NS, -1)]).T.reshape(DT, P, T)
    w_mix = blocks(v["hgrn_w_in"][0])
    order = [[8 + t, t, 16 + t, 24 + t] for t in range(HEADS)]
    w_mix = w_mix[np.array(order).reshape(-1)]
    gains = np.zeros((P, N_GAIN), np.float32)
    gains[:, G_MIX:G_MIX + 16] = vec(v["norm_mix"])
    gains[:, G_FFN:G_FFN + 16] = vec(v["norm_ffn"])
    gains[:, G_KV:G_KV + 8] = vec(v["kv_norm"])
    gains[:, G_ON] = v["hgrn_onorm"][0]
    gains[:, G_K] = np.tile(v["k_norm"], 2)
    gains[:, G_Q] = np.tile(v["q_norm"][0], 2)
    gains[0:FOX, G_BF] = v["fox_b_f"]
    gains[:, G_CW:G_CB] = vec(v["ffn_conv_w"])
    gains[:, G_CB:] = vec(v["ffn_conv_b"])
    cc, masks = consts()
    wkv = v["w_kvf"]
    wl = np.zeros((wkv.shape[0], P), np.float32)
    wl[:, 0:FOX] = wkv[:, 2048:]
    wk, wv = blocks(wkv[:, 0:1024]), blocks(wkv[:, 1024:2048])
    qg = blocks(v["fox_w_qg"][0])
    arrays = {
        "x": x, "gains": gains, "consts": cc, "masks": masks.reshape(P, 8 * P),
        "w_mix": w_mix, "w_o0": blocks(v["hgrn_w_o"][0]), "w_o1": blocks(v["fox_w_o"][0]),
        "w_kv": np.concatenate([blocks(wl)] + [w[p:p + 1] for p in range(8) for w in (wk, wv)]),
        "w_qg": np.concatenate([qg[8 * j + p:8 * j + p + 1] for p in range(8) for j in (0, 1)]),
        "s0": v["state_hgrn"][0].transpose(1, 2, 0, 3).reshape(HEADS, P, NSEQ * P),
        "conv_in": v["state_conv"].reshape(2, NSEQ, 2, FT, P).transpose(0, 4, 3, 1, 2).reshape(2, P, FT * 16),
        "pages": v["page_table"].reshape(1, -1),
        "cache_k": v["cache_k"].reshape(n_phys, P, 8, P).transpose(0, 3, 2, 1).reshape(n_phys, P, 8 * P),
        "cache_v": v["cache_v"].reshape(n_phys, P, 8 * P),
        "cache_f": v["cache_logf"].transpose(0, 2, 1),
    }
    for layer in range(2):
        w = blocks(v["ffn_w_in"][layer])
        arrays[f"w_fi{layer}"] = np.stack([w[:FT], w[FT:]], 1).reshape(2 * FT, P, 1024)
        arrays[f"w_fo{layer}"] = blocks(v["ffn_w_out"][layer])
    i = np.arange(P)
    neg = np.zeros((P, 4 * P + NSEQ * NS), np.float32)
    neg[:, 0:P] = np.eye(P)
    neg[:, P:2 * P] = np.where(i[None, :] > i[:, None], -1e30, 0.0)
    s_, n_ = np.arange(NS), np.arange(NSEQ)
    own = (s_[None, None, :] // 8 == n_[None, :, None]) & (s_[None, None, :] % 8 <= i[:, None, None] % 8)
    neg[:, 2 * P:2 * P + NSEQ * NS] = np.where(own, 0.0, -1e30).reshape(P, NSEQ * NS)
    for a in range(2):
        neg[2 * a:2 * a + 2, (a - 2) * P:(a - 1) * P or None] = -1.0
    arrays["att_masks"] = neg
    arrays = {f"{k}_in": np.ascontiguousarray(a) for k, a in arrays.items()}
    outs = {"y": (DT, P, T), "k_out": (DT, P, T), "v_out": (DT, P, T), "f_out": (FOX, T), "hgrn_p": (HEADS, P, P),
            "hgrn_s": (HEADS, P, NSEQ * P), "conv_out": (2, P, FT * 18)}

    nc = bacc.Bacc("TRN2", target_bir_lowering=False, num_devices=1)
    d = {k[:-3]: nc.dram_tensor(k, a.shape, mybir.dt.from_np(a.dtype), kind="ExternalInput").ap() for k, a in arrays.items()}
    d |= {k: nc.dram_tensor(f"{k}_out", s, F32, kind="ExternalOutput").ap() for k, s in outs.items()}
    d["c_row"] = nc.dram_tensor("c_row", (FOX, 2, SEQ), F32R, kind="Internal").ap()
    build(nc, d)
    r = run_bass_kernel_spmd(nc, [arrays], core_ids=[0]).results[0]
    r = {k: r[f"{k}_out"] for k in outs}

    def tokens(a):
        a = a.reshape(-1, T).T
        return a[:SEQ], a[SEQ:]

    yp, ys = tokens(r["y"])
    kp, ks = tokens(r["k_out"])
    vp, vs = tokens(r["v_out"])
    fp, fs = tokens(r["f_out"])
    co = r["conv_out"].reshape(2, P, FT, 18)
    return (yp.reshape(1, SEQ, 1024), ys.reshape(NSEQ, DSEQ, 1024),
            kp.reshape(1, SEQ, FOX, 64), vp.reshape(1, SEQ, FOX, 64), fp.reshape(1, SEQ, FOX),
            ks.reshape(NSEQ, DSEQ, FOX, 64), vs.reshape(NSEQ, DSEQ, FOX, 64), fs.reshape(NSEQ, DSEQ, FOX),
            r["hgrn_p"].reshape(1, 1, HEADS, P, P),
            r["hgrn_s"].reshape(HEADS, P, NSEQ, P).transpose(2, 0, 1, 3)[None],
            co[..., 0:2].transpose(0, 3, 2, 1).reshape(2, 1, 2, FT * P),
            co[..., 2:].reshape(2, P, FT, NSEQ, 2).transpose(0, 3, 4, 2, 1).reshape(2, NSEQ, 2, FT * P))
```
